# Optimizing a Trainium2 kernel written in Bass

```python
import jax, jax.numpy as jnp
from jax import lax
import numpy as np

D_MODEL = 1024
BATCH = 1
SEQ = 256
DEPTH = 1

HEAD_DIM = 128
DSA_HEADS = 4
MOBA_HEADS = 4
IDX_HEADS = 8
IDX_DIM = 64
DSA_TOPK_MAX = 256
MOBA_BLOCK = 256
MOBA_TOPK = 3
D_FF = -(-8 * D_MODEL // 768) * 256
ROPE_THETA = 10000.0
EPS = 1e-6
NEG = -1e30
DSA_Q_BLOCK = 128
MOBA_Q_BLOCK = 32
DSA_W = DSA_HEADS * HEAD_DIM
MOBA_W = MOBA_HEADS * HEAD_DIM
IN_SIZES = (DSA_W, DSA_W, DSA_W, IDX_HEADS * IDX_DIM, IDX_DIM, IDX_HEADS,
            MOBA_W, MOBA_W, MOBA_W, D_MODEL, D_MODEL)
IN_W = sum(IN_SIZES)
N_MOD = 6


def rms_norm(x, gain):
    xf = x.astype(jnp.float32)
    y = xf * lax.rsqrt(jnp.mean(xf * xf, axis=-1, keepdims=True) + EPS)
    return (y * gain.astype(jnp.float32)).astype(x.dtype)

def rope_tables(seq, dim):
    inv = ROPE_THETA ** (-jnp.arange(0, dim, 2, dtype=jnp.float32) / dim)
    ang = jnp.arange(seq, dtype=jnp.float32)[:, None] * inv[None, :]
    return jnp.cos(ang)[:, None, :], jnp.sin(ang)[:, None, :]

def apply_rope(x, cos, sin):
    x1, x2 = jnp.split(x.astype(jnp.float32), 2, axis=-1)
    return jnp.concatenate([x1 * cos - x2 * sin, x2 * cos + x1 * sin], axis=-1).astype(x.dtype)

def dsa_attention(q, k, v, qi, ki, wi):
    B, S, H, Dh = q.shape
    topk = min(DSA_TOPK_MAX, S // 4)
    nq = S // DSA_Q_BLOCK
    scale = Dh ** -0.5
    key_pos = jnp.arange(S)
    bi = jnp.arange(B)[:, None, None]

    def chunks(a):
        return jnp.moveaxis(a.reshape(a.shape[0], nq, DSA_Q_BLOCK, *a.shape[2:]), 1, 0)

    def block(args):
        qb, qib, wib, t = args
        logits = jnp.einsum('bqhd,bsd->bqhs', qib, ki).astype(jnp.float32)
        score = jnp.einsum('bqh,bqhs->bqs', wib.astype(jnp.float32), jax.nn.relu(logits))
        score = jnp.where((key_pos[None, :] <= t[:, None])[None], score, NEG)
        _, sel = lax.top_k(score, topk)
        ks = k[bi, sel]
        vs = v[bi, sel]
        s = jnp.einsum('bqhd,bqkhd->bhqk', qb, ks).astype(jnp.float32) * scale
        valid = sel <= t[None, :, None]
        s = jnp.where(valid[:, None], s, NEG)
        p = jax.nn.softmax(s, axis=-1).astype(v.dtype)
        return jnp.einsum('bhqk,bqkhd->bqhd', p, vs)

    t_c = jnp.arange(S).reshape(nq, DSA_Q_BLOCK)
    out = lax.map(block, (chunks(q), chunks(qi), chunks(wi), t_c))
    return jnp.moveaxis(out, 0, 1).reshape(B, S, H * Dh)

def moba_attention(q, k, v):
    B, S, H, Dh = q.shape
    nb = -(-S // MOBA_BLOCK)
    pad = nb * MOBA_BLOCK - S
    scale = Dh ** -0.5
    qh = q.transpose(0, 2, 1, 3)
    padw = ((0, 0), (0, 0), (0, pad), (0, 0))
    kh = jnp.pad(k.transpose(0, 2, 1, 3), padw).reshape(B, H, nb, MOBA_BLOCK, Dh)
    vh = jnp.pad(v.transpose(0, 2, 1, 3), padw).reshape(B, H, nb, MOBA_BLOCK, Dh)
    own = (jnp.arange(S) // MOBA_BLOCK).astype(jnp.int32)
    own_b = jnp.broadcast_to(own[:, None], (B, H, S, 1))
    n_sel = min(MOBA_TOPK, nb - 1)
    if n_sel > 0:
        kmean = jnp.mean(kh.astype(jnp.float32), axis=3)
        gate = jnp.einsum('bhsd,bhnd->bhsn', qh.astype(jnp.float32), kmean)
        past = jnp.arange(nb)[None, :] < own[:, None]
        gate = jnp.where(past, gate, NEG)
        _, sel = lax.top_k(gate, n_sel)
        blocks = jnp.concatenate([sel.astype(jnp.int32), own_b], axis=-1)
        bvalid = jnp.concatenate([sel < own[:, None], jnp.ones((B, H, S, 1), bool)], axis=-1)
    else:
        blocks = own_b
        bvalid = jnp.ones((B, H, S, 1), bool)
    nq = S // MOBA_Q_BLOCK
    bi = jnp.arange(B)[:, None, None, None]
    hi = jnp.arange(H)[None, :, None, None]
    offs = jnp.arange(MOBA_BLOCK)

    def chunks(a):
        return jnp.moveaxis(a.reshape(B, H, nq, MOBA_Q_BLOCK, *a.shape[3:]), 2, 0)

    def block(args):
        qb, bl, bv, t = args
        kg = kh[bi, hi, bl]
        vg = vh[bi, hi, bl]
        s = jnp.einsum('bhqd,bhqnkd->bhqnk', qb, kg).astype(jnp.float32) * scale
        kpos = bl[..., None] * MOBA_BLOCK + offs
        mask = bv[..., None] & (kpos <= t[:, None, None])
        s = jnp.where(mask, s, NEG)
        shp = s.shape
        p = jax.nn.softmax(s.reshape(shp[0], shp[1], shp[2], -1), axis=-1).reshape(shp).astype(v.dtype)
        return jnp.einsum('bhqnk,bhqnkd->bhqd', p, vg)

    t_c = jnp.arange(S).reshape(nq, MOBA_Q_BLOCK)
    out = lax.map(block, (chunks(qh), chunks(blocks), chunks(bvalid), t_c))
    out = jnp.moveaxis(out, 0, 2).reshape(B, H, S, Dh)
    return out.transpose(0, 2, 1, 3).reshape(B, S, H * Dh)

def first_inputs(seed: int = 0) -> dict:
    key = jax.random.key(seed)
    ks = jax.random.split(key, 16)
    f32 = jnp.float32

    def w(k, shape, fan_in):
        return jax.random.normal(k, shape, f32) * fan_in ** -0.5

    def gain(k, shape):
        return 1.0 + 0.02 * jax.random.normal(k, shape, f32)

    return {
        "x": jax.random.normal(ks[0], (BATCH, SEQ, D_MODEL), f32),
        "c": jax.random.normal(ks[1], (BATCH, D_MODEL), f32),
        "w_mod": w(ks[2], (DEPTH, D_MODEL, N_MOD * D_MODEL), D_MODEL),
        "b_mod": 0.02 * jax.random.normal(ks[3], (DEPTH, N_MOD * D_MODEL), f32),
        "g_mix_norm": gain(ks[4], (DEPTH, D_MODEL)),
        "g_ffn_norm": gain(ks[5], (DEPTH, D_MODEL)),
        "w_in": w(ks[6], (DEPTH, D_MODEL, IN_W), D_MODEL),
        "g_q_dsa": gain(ks[7], (DEPTH, HEAD_DIM)),
        "g_k_dsa": gain(ks[8], (DEPTH, HEAD_DIM)),
        "g_q_moba": gain(ks[9], (DEPTH, HEAD_DIM)),
        "g_k_moba": gain(ks[10], (DEPTH, HEAD_DIM)),
        "w_br_dsa": w(ks[11], (DEPTH, DSA_W, D_MODEL), DSA_W),
        "w_br_moba": w(ks[12], (DEPTH, MOBA_W, D_MODEL), MOBA_W),
        "w_out": w(ks[13], (DEPTH, D_MODEL, D_MODEL), D_MODEL),
        "w_gate_up": w(ks[14], (DEPTH, D_MODEL, 2 * D_FF), D_MODEL),
        "w_down": w(ks[15], (DEPTH, D_FF, D_MODEL), D_FF),
    }

def first_block(x, c, w_mod, b_mod, g_mix_norm, g_ffn_norm, w_in, g_q_dsa, g_k_dsa,
              g_q_moba, g_k_moba, w_br_dsa, w_br_moba, w_out, w_gate_up, w_down):
    B, S, _ = x.shape
    cos_h, sin_h = rope_tables(S, HEAD_DIM)
    cos_i, sin_i = rope_tables(S, IDX_DIM)
    split_at = np.cumsum(IN_SIZES)[:-1].tolist()
    idx_w_scale = (IDX_HEADS ** -0.5) * (IDX_DIM ** -0.5)
    for l in range(DEPTH):
        mod = jax.nn.silu(c) @ w_mod[l] + b_mod[l]
        sh_m, sc_m, gt_m, sh_f, sc_f, gt_f = [m[:, None, :] for m in jnp.split(mod, N_MOD, axis=-1)]

        h = rms_norm(x, g_mix_norm[l]) * (1.0 + sc_m) + sh_m
        proj = h @ w_in[l]
        (q_a, k_a, v_a, q_i, k_i, w_i, q_b, k_b, v_b, gate_a, gate_b) = jnp.split(proj, split_at, axis=-1)
        q_a = apply_rope(rms_norm(q_a.reshape(B, S, DSA_HEADS, HEAD_DIM), g_q_dsa[l]), cos_h, sin_h)
        k_a = apply_rope(rms_norm(k_a.reshape(B, S, DSA_HEADS, HEAD_DIM), g_k_dsa[l]), cos_h, sin_h)
        v_a = v_a.reshape(B, S, DSA_HEADS, HEAD_DIM)
        q_i = apply_rope(q_i.reshape(B, S, IDX_HEADS, IDX_DIM), cos_i, sin_i)
        k_i = apply_rope(k_i[:, :, None, :], cos_i, sin_i)[:, :, 0, :]
        w_i = w_i * idx_w_scale
        o_a = dsa_attention(q_a, k_a, v_a, q_i, k_i, w_i)

        q_b = apply_rope(rms_norm(q_b.reshape(B, S, MOBA_HEADS, HEAD_DIM), g_q_moba[l]), cos_h, sin_h)
        k_b = apply_rope(rms_norm(k_b.reshape(B, S, MOBA_HEADS, HEAD_DIM), g_k_moba[l]), cos_h, sin_h)
        v_b = v_b.reshape(B, S, MOBA_HEADS, HEAD_DIM)
        o_b = moba_attention(q_b, k_b, v_b)

        merged = (jax.nn.sigmoid(gate_a) * (o_a @ w_br_dsa[l])
                  + jax.nn.sigmoid(gate_b) * (o_b @ w_br_moba[l]))
        x = x + gt_m * (merged @ w_out[l])

        h = rms_norm(x, g_ffn_norm[l]) * (1.0 + sc_f) + sh_f
        g_ff, u_ff = jnp.split(h @ w_gate_up[l], 2, axis=-1)
        x = x + gt_f * ((jax.nn.silu(g_ff) * u_ff) @ w_down[l])
    return x


DEPTH_2 = 2

N_A_LAYERS = DEPTH_2 // 2
N_B_LAYERS = DEPTH_2 - N_A_LAYERS
D_FF_2 = 2816
CONV_WIDTH = 3
N_HEADS = 16
HEAD_DIM_2 = D_MODEL // N_HEADS
N_KV_GROUPS = 4
HEADS_PER_GROUP = N_HEADS // N_KV_GROUPS
CMP_BLOCK = 32
CMP_STRIDE = 16
CMP_HIDDEN = 4 * HEAD_DIM_2
SEL_BLOCK = 64
N_SELECT = 16
WINDOW = 512
N_BRANCH = 3
N_KV_SLOTS = 6
QUERY_CHUNK = 32
FORCE_SCORE = 1e9
MASK_SCORE = -1e30


def _rmsnorm(x, g):
    xf = x.astype(jnp.float32)
    y = xf * lax.rsqrt(jnp.mean(xf * xf, axis=-1, keepdims=True) + EPS)
    return (y * g.astype(jnp.float32)).astype(x.dtype)

def _swiglu(x, w_gate_up, w_down):
    a, b = jnp.split(x @ w_gate_up, 2, axis=-1)
    return (jax.nn.silu(a) * b) @ w_down

def _short_conv(x, w_in, conv_w, w_out):
    b_gate, c_gate, u = jnp.split(x @ w_in, 3, axis=-1)
    v = c_gate * u
    conv = lax.conv_general_dilated(
        v, conv_w[:, None, :], window_strides=(1,), padding=[(CONV_WIDTH - 1, 0)],
        dimension_numbers=("NWC", "WIO", "NWC"), feature_group_count=D_MODEL)
    return (b_gate * conv) @ w_out

def _compress(x_raw, pos, w1, b1, w2):
    s = x_raw.shape[2]
    n_cmp = (s - CMP_BLOCK) // CMP_STRIDE + 1
    idx = np.arange(n_cmp)[:, None] * CMP_STRIDE + np.arange(CMP_BLOCK)[None, :]
    blocks = x_raw[:, :, idx] + pos
    flat = blocks.reshape(blocks.shape[:3] + (CMP_BLOCK * HEAD_DIM_2,))
    return jax.nn.gelu(flat @ w1 + b1) @ w2

def _shared_kv(h, kv_norm, kv_w, cmp_pos, cmp_w1, cmp_b1, cmp_w2, k_norm):
    b, s, _ = h.shape
    kv = (_rmsnorm(h, kv_norm) @ kv_w).reshape(b, s, N_KV_SLOTS, N_KV_GROUPS, HEAD_DIM_2)
    kv = jnp.transpose(kv, (2, 0, 3, 1, 4))
    k_cmp = _rmsnorm(_compress(kv[0], cmp_pos[0], cmp_w1[0], cmp_b1[0], cmp_w2[0]), k_norm[0])
    v_cmp = _compress(kv[1], cmp_pos[1], cmp_w1[1], cmp_b1[1], cmp_w2[1])
    n_blk = s // SEL_BLOCK
    k_sel = _rmsnorm(kv[2], k_norm[1]).reshape(b, N_KV_GROUPS, n_blk, SEL_BLOCK, HEAD_DIM_2)
    v_sel = kv[3].reshape(b, N_KV_GROUPS, n_blk, SEL_BLOCK, HEAD_DIM_2)
    pad = ((0, 0), (0, 0), (WINDOW, 0), (0, 0))
    k_win = jnp.pad(_rmsnorm(kv[4], k_norm[2]), pad)
    v_win = jnp.pad(kv[5], pad)
    return (k_cmp, v_cmp, k_sel, v_sel, k_win, v_win)

def _softmax_f32(logits, mask):
    return jax.nn.softmax(jnp.where(mask, logits, MASK_SCORE), axis=-1)

def _nsa(x, w_qg, q_norm, w_o, k_cmp, v_cmp, k_sel, v_sel, k_win, v_win):
    b, s, _ = x.shape
    n_chunk = s // QUERY_CHUNK
    n_cmp = k_cmp.shape[2]
    n_blk = k_sel.shape[2]
    n_sel = min(N_SELECT, n_blk)
    scale = HEAD_DIM_2 ** -0.5

    proj = x @ w_qg
    q = _rmsnorm(proj[..., :N_HEADS * HEAD_DIM_2].reshape(b, s, N_HEADS, HEAD_DIM_2), q_norm)
    gate = jax.nn.sigmoid(proj[..., N_HEADS * HEAD_DIM_2:].astype(jnp.float32))
    q = q.reshape(b, n_chunk, QUERY_CHUNK, N_KV_GROUPS, HEADS_PER_GROUP, HEAD_DIM_2)
    q = q.transpose(1, 0, 3, 4, 2, 5)
    gate = gate.reshape(b, n_chunk, QUERY_CHUNK, N_KV_GROUPS, HEADS_PER_GROUP, N_BRANCH)
    gate = gate.transpose(1, 0, 3, 4, 2, 5)

    cmp_start = np.arange(n_cmp) * CMP_STRIDE
    cmp_end = cmp_start + CMP_BLOCK - 1
    blk_start = np.arange(n_blk) * SEL_BLOCK
    overlap = ((cmp_start[:, None] < blk_start[None, :] + SEL_BLOCK)
               & (cmp_start[:, None] + CMP_BLOCK > blk_start[None, :])).astype(np.float32)
    gather_blocks = jax.vmap(jax.vmap(lambda kb, ib: kb[ib]))
    blk_ids = jnp.arange(n_blk)

    def chunk_fn(args):
        c, qc, gc = args
        t = c * QUERY_CHUNK + jnp.arange(QUERY_CHUNK)
        logits = jnp.einsum("bghtd,bgnd->bghtn", qc, k_cmp).astype(jnp.float32) * scale
        valid = cmp_end[None, :] <= t[:, None]
        p_cmp = _softmax_f32(logits, valid) * valid
        o_cmp = jnp.einsum("bghtn,bgnd->bghtd", p_cmp.astype(v_cmp.dtype), v_cmp)
        imp = jnp.einsum("bghtn,nj->bgtj", p_cmp, overlap)
        cur = (t // SEL_BLOCK)[:, None]
        forced = (blk_ids[None] == 0) | (blk_ids[None] == cur) | (blk_ids[None] == cur - 1)
        imp = jnp.where(forced, FORCE_SCORE, imp)
        imp = jnp.where(blk_ids[None] > cur, MASK_SCORE, imp)
        _, idx = lax.top_k(imp, n_sel)
        ks = gather_blocks(k_sel, idx).reshape(b, N_KV_GROUPS, QUERY_CHUNK, n_sel * SEL_BLOCK, HEAD_DIM_2)
        vs = gather_blocks(v_sel, idx).reshape(b, N_KV_GROUPS, QUERY_CHUNK, n_sel * SEL_BLOCK, HEAD_DIM_2)
        kpos = (idx[..., None] * SEL_BLOCK + jnp.arange(SEL_BLOCK)).reshape(
            b, N_KV_GROUPS, QUERY_CHUNK, n_sel * SEL_BLOCK)
        smask = (kpos <= t[:, None])[:, :, None]
        logits = jnp.einsum("bghtd,bgtkd->bghtk", qc, ks).astype(jnp.float32) * scale
        p_sel = _softmax_f32(logits, smask)
        o_sel = jnp.einsum("bghtk,bgtkd->bghtd", p_sel.astype(vs.dtype), vs)
        start = c * QUERY_CHUNK
        kw = lax.dynamic_slice_in_dim(k_win, start, WINDOW + QUERY_CHUNK, axis=2)
        vw = lax.dynamic_slice_in_dim(v_win, start, WINDOW + QUERY_CHUNK, axis=2)
        wpos = start - WINDOW + jnp.arange(WINDOW + QUERY_CHUNK)
        wmask = ((wpos[None] <= t[:, None]) & (wpos[None] > t[:, None] - WINDOW)
                 & (wpos[None] >= 0))
        logits = jnp.einsum("bghtd,bgkd->bghtk", qc, kw).astype(jnp.float32) * scale
        p_win = _softmax_f32(logits, wmask)
        o_win = jnp.einsum("bghtk,bgkd->bghtd", p_win.astype(vw.dtype), vw)
        out = gc[..., 0:1] * o_cmp + gc[..., 1:2] * o_sel + gc[..., 2:3] * o_win
        return out.astype(qc.dtype)

    outs = lax.map(chunk_fn, (jnp.arange(n_chunk), q, gate))
    o = outs.transpose(1, 0, 4, 2, 3, 5).reshape(b, s, N_HEADS * HEAD_DIM_2)
    return o @ w_o

def second_inputs(seed: int = 0) -> dict:
    key = jax.random.key(seed)
    ks = jax.random.split(key, 20)
    nrm = lambda k, shape, scale: jax.random.normal(k, shape, jnp.float32) * scale
    gain = lambda k, shape: 1.0 + 0.02 * jax.random.normal(k, shape, jnp.float32)
    qg_width = N_HEADS * HEAD_DIM_2 + N_BRANCH * N_HEADS
    return {
        "x": nrm(ks[0], (BATCH, SEQ, D_MODEL), 1.0),
        "ffn_norm": gain(ks[1], (DEPTH_2, 2, D_MODEL)),
        "ffn_w_gate_up": nrm(ks[2], (DEPTH_2, 2, D_MODEL, 2 * D_FF_2), D_MODEL ** -0.5),
        "ffn_w_down": nrm(ks[3], (DEPTH_2, 2, D_FF_2, D_MODEL), D_FF_2 ** -0.5),
        "mix_norm": gain(ks[4], (DEPTH_2, D_MODEL)),
        "conv_w_in": nrm(ks[5], (N_A_LAYERS, D_MODEL, 3 * D_MODEL), D_MODEL ** -0.5),
        "conv_w": nrm(ks[6], (N_A_LAYERS, CONV_WIDTH, D_MODEL), CONV_WIDTH ** -0.5),
        "conv_w_out": nrm(ks[7], (N_A_LAYERS, D_MODEL, D_MODEL), D_MODEL ** -0.5),
        "kv_norm": gain(ks[8], (D_MODEL,)),
        "kv_w": nrm(ks[9], (D_MODEL, N_KV_SLOTS * N_KV_GROUPS * HEAD_DIM_2), D_MODEL ** -0.5),
        "cmp_pos": nrm(ks[10], (2, CMP_BLOCK, HEAD_DIM_2), 0.1),
        "cmp_w1": nrm(ks[11], (2, CMP_BLOCK * HEAD_DIM_2, CMP_HIDDEN), (CMP_BLOCK * HEAD_DIM_2) ** -0.5),
        "cmp_b1": nrm(ks[12], (2, CMP_HIDDEN), 0.01),
        "cmp_w2": nrm(ks[13], (2, CMP_HIDDEN, HEAD_DIM_2), CMP_HIDDEN ** -0.5),
        "k_norm": gain(ks[14], (N_BRANCH, HEAD_DIM_2)),
        "nsa_w_qg": nrm(ks[15], (N_B_LAYERS, D_MODEL, qg_width), D_MODEL ** -0.5),
        "q_norm": gain(ks[16], (N_B_LAYERS, HEAD_DIM_2)),
        "nsa_w_o": nrm(ks[17], (N_B_LAYERS, N_HEADS * HEAD_DIM_2, D_MODEL), (N_HEADS * HEAD_DIM_2) ** -0.5),
    }

def second_block(x, ffn_norm, ffn_w_gate_up, ffn_w_down, mix_norm, conv_w_in, conv_w, conv_w_out,
              kv_norm, kv_w, cmp_pos, cmp_w1, cmp_b1, cmp_w2, k_norm, nsa_w_qg, q_norm, nsa_w_o):
    h = x
    shared = None
    for layer in range(DEPTH_2):
        h = h + 0.5 * _swiglu(_rmsnorm(h, ffn_norm[layer, 0]), ffn_w_gate_up[layer, 0], ffn_w_down[layer, 0])
        hn = _rmsnorm(h, mix_norm[layer])
        if layer < N_A_LAYERS:
            h = h + _short_conv(hn, conv_w_in[layer], conv_w[layer], conv_w_out[layer])
        else:
            i = layer - N_A_LAYERS
            h = h + _nsa(hn, nsa_w_qg[i], q_norm[i], nsa_w_o[i], *shared)
        h = h + 0.5 * _swiglu(_rmsnorm(h, ffn_norm[layer, 1]), ffn_w_gate_up[layer, 1], ffn_w_down[layer, 1])
        if layer == N_A_LAYERS - 1:
            shared = _shared_kv(h, kv_norm, kv_w, cmp_pos, cmp_w1, cmp_b1, cmp_w2, k_norm)
    return h


def setup_inputs(seed=0):
    out = dict(first_inputs(seed))
    for name, value in second_inputs(seed + 1).items():
        if name != "x":
            out[name + "_2"] = value
    return out


def reference(
    x, c, w_mod, b_mod, g_mix_norm, g_ffn_norm, w_in, g_q_dsa, g_k_dsa, g_q_moba, g_k_moba,
    w_br_dsa, w_br_moba, w_out, w_gate_up, w_down, ffn_norm_2, ffn_w_gate_up_2, ffn_w_down_2,
    mix_norm_2, conv_w_in_2, conv_w_2, conv_w_out_2, kv_norm_2, kv_w_2, cmp_pos_2, cmp_w1_2,
    cmp_b1_2, cmp_w2_2, k_norm_2, nsa_w_qg_2, q_norm_2, nsa_w_o_2,
):
    x = first_block(
        x, c, w_mod, b_mod, g_mix_norm, g_ffn_norm, w_in, g_q_dsa, g_k_dsa, g_q_moba, g_k_moba,
        w_br_dsa, w_br_moba, w_out, w_gate_up, w_down,
    )
    return second_block(
        x, ffn_norm_2, ffn_w_gate_up_2, ffn_w_down_2, mix_norm_2, conv_w_in_2, conv_w_2,
        conv_w_out_2, kv_norm_2, kv_w_2, cmp_pos_2, cmp_w1_2, cmp_b1_2, cmp_w2_2, k_norm_2,
        nsa_w_qg_2, q_norm_2, nsa_w_o_2,
    )


_drawn_inputs = setup_inputs


def setup_inputs(seed=0):
    import zlib

    import numpy as np

    out = dict(_drawn_inputs(seed))
    spreads = {}
    factors = {'g_mix_norm': 3.996,
     'g_ffn_norm': 2.802,
     'g_q_dsa': 8.0,
     'g_k_dsa': 8.0,
     'g_q_moba': 8.0,
     'g_k_moba': 8.0,
     'ffn_norm_2': 4.331,
     'kv_norm_2': 8.0,
     'cmp_pos_2': 3.219,
     'cmp_b1_2': 61.434,
     'k_norm_2': 8.0,
     'q_norm_2': 8.0}
    for name, (base, spread) in spreads.items():
        noise = np.random.default_rng([zlib.crc32(name.encode()), seed]).standard_normal(out[name].shape)
        drawn = base * np.exp(spread * noise) if base else spread * noise
        out[name] = __import__('jax').numpy.asarray(drawn.astype(out[name].dtype))
    for name, factor in factors.items():
        out[name] = (out[name] * factor).astype(out[name].dtype)
    return out
```

```python
from contextlib import ExitStack

import numpy as np

import concourse.bass as bass
from concourse import mybir

ALU = mybir.AluOpType
ACT = mybir.ActivationFunctionType
F32 = mybir.dt.float32
F32R = mybir.dt.float32r
AX = mybir.AxisListType

P = 128
T = 256
TT = T // P
D = 1024
KT = D // P
FF = 2816
GC = 256
NJ = FF // GC
UNIT = 2048
RING = 3
HD = 128
NH = 4
IH, ID = 8, 64
TOPK = 64
NQ, DH, NG = 16, 64, 4
CB, CS = 32, 16
NC = (T - CB) // CS + 1
EPS = 1e-6
NEG = -1e30
TAKEN = -3e38
HI_SCALE = (IH ** -0.5) * (ID ** -0.5)

C_ID, C_ONE, C_COSH, C_SINH = 0, 128, 256, 512
C_COSI, C_SINI, C_MASK, C_CM, C_CV, C_END = 768, 896, 1024, 1280, 1312, 1344


def constant_table():
    t = np.zeros((P, C_END), np.float32)
    t[:, C_ID:C_ID + P] = np.eye(P, dtype=np.float32)
    t[:, C_ONE:C_ONE + P] = 1.0
    for dim, at_cos, at_sin in ((HD, C_COSH, C_SINH), (ID, C_COSI, C_SINI)):
        inv = np.float32(10000.0) ** (-np.arange(0, dim, 2, dtype=np.float32) / np.float32(dim))
        ang = np.arange(T, dtype=np.float32)[:, None] * inv[None, :].astype(np.float32)
        cos, sin = np.cos(ang).astype(np.float32), np.sin(ang).astype(np.float32)
        for tt in range(TT):
            rows = slice(tt * P, (tt + 1) * P)
            t[:, at_cos + tt * dim:at_cos + (tt + 1) * dim] = np.concatenate([cos[rows], cos[rows]], 1)
            t[:, at_sin + tt * dim:at_sin + (tt + 1) * dim] = np.concatenate([-sin[rows], sin[rows]], 1)
    q, k = np.arange(P)[:, None], np.arange(P)[None, :]
    t[:, C_MASK + P:C_MASK + 2 * P] = np.where(k <= q, 0.0, NEG)
    end = np.arange(NC) * CS + CB - 1
    for tt in range(TT):
        ok = end[None, :] <= (np.arange(P) + tt * P)[:, None]
        t[:, C_CM + tt * 16:C_CM + tt * 16 + NC] = np.where(ok, 0.0, -NEG)
        t[:, C_CV + tt * 16:C_CV + tt * 16 + NC] = ok
    return t


def make_plan():
    plan, units = [], []

    def add(kind, **a):
        item = dict(a, kind=kind)
        plan.append(item)
        return item

    def lin(stage, chunk, parts, extra=(), before_evac=()):
        for part in range(parts):
            add("lin", stage=stage, chunk=chunk, part=part, parts=parts, unit=len(units))
            units.append((stage, chunk, part))
            for e in extra[part:part + 1]:
                for a in e:
                    plan.extend(a)
        plan.extend(before_evac)
        add("evac", stage=stage, chunk=chunk)

    def tgroup(stage, n, **a):
        return [dict(a, kind="tp", stage=stage, g=g) for g in range(n)]

    def mods(m):
        add("mod", m=m, half=0)
        add("mod", m=m, half=1)
        add("tp", stage="mod", g=m)

    def ffn(f, stage, norm, last=False):
        add("ffn", f=f, stage=stage, norm=norm, last=last, unit=len(units))
        for j in range(NJ + 1):
            if j < NJ:
                units.extend([(stage, j, 0), (stage, j, 1)])
            if j > 0:
                units.append((stage + "_d", j - 1, 0))

    def norm(n, plain):
        if plain:
            plan.extend(tgroup("norm", 4, norm=n))
            add("square")
        else:
            add("square")
            add("scale_x", norm=n)
            plan.extend(tgroup("normf", 4, norm=n))

    def attention(items, slots):
        steps = []
        for i in range(len(items) + 2):
            s = []
            if i < len(items):
                s += [dict(items[i], kind="qk"), dict(items[i], kind="sm")]
            if 1 <= i <= len(items):
                s.append(dict(items[i - 1], kind="tp", stage="p", g=0))
            if i >= 2:
                s.append(dict(items[i - 2], kind="pv"))
            steps.append(s)
        return [steps[k * len(steps) // slots:(k + 1) * len(steps) // slots] for k in range(slots)]

    add("init")
    for m in range(4):
        mods(m)
    add("mod_a", norm=0)
    norm(0, False)
    lin("ki", 0, 1)
    mods(4)
    lin("qi", 0, 2, before_evac=tgroup("ki", 1))
    mods(5)
    lin("qb", 0, 2, before_evac=tgroup("qi", 2))
    mods(6)
    lin("kb", 0, 2, before_evac=tgroup("qb", 2))
    mods(7)
    lin("vb", 0, 2, before_evac=tgroup("kb", 2))
    pieces = attention([dict(b="moba", h=h, tt=tt) for h in range(NH) for tt in range(TT)], 4)
    index = [[dict(kind="ix", tt=tt, pair=pr) for pr in range(4)] for tt in range(TT)]
    lin("ga", 0, 2, [pieces[0], pieces[1]])
    lin("ga", 1, 2, [pieces[2], pieces[3]])
    lin("qa", 0, 2, [[index[0]], [index[1]]])
    add("topk", tt=0)
    mods(8)
    lin("ka", 0, 2, before_evac=tgroup("qa", 2))
    add("topk", tt=1)
    mods(9)
    lin("va", 0, 2, before_evac=tgroup("ka", 2))
    pieces = attention([dict(b="dsa", h=h, tt=tt) for h in range(NH) for tt in range(TT)], 4)
    lin("gb", 0, 2, [pieces[0], pieces[1]])
    lin("gb", 1, 2, [pieces[2], pieces[3]])
    add("sigmoid")
    plan.extend(tgroup("o", 4))
    mods(10)
    for c in range(2):
        lin("ba", c, 1)
    for c in range(2):
        lin("bb", c, 1)
    mods(11)
    add("mod_a", norm=1)
    plan.extend(tgroup("merged", 4))
    for c in range(2):
        lin("out1", c, 2)
    norm(1, False)
    ffn(0, "f0", 1)
    norm(2, True)
    ffn(1, "f1", 2)
    norm(3, True)
    for j in range(4):
        add("glu", j=j, unit=len(units))
        units.extend([("cv", j, 0), ("cv", j, 1)])
    for c in range(2):
        lin("cb", c, 2)
    add("conv")
    plan.extend(tgroup("cb", 4))
    for c in range(2):
        lin("co", c, 2)
    norm(4, True)
    ffn(2, "f2", 4)
    norm(5, True)
    for c in range(3):
        lin("kv", c, 2, before_evac=[dict(kind="tp", stage="kvt", g=g, c=c - 1) for g in range([0, 4, 2][c])])
    norm(6, True)
    plan.extend([dict(kind="tp", stage="kvt", g=g, c=2) for g in range(2)])
    ffn(3, "f3", 6)
    for s in range(2):
        add("xp", s=s)
        lin("cm", s, 2)
        plan.append(dict(kind="tp", stage="hc", g=0, c=s))
        add("cmp", s=s)
    plan.append(dict(kind="tp", stage="kc", g=0))
    norm(7, True)
    lin("qg", 0, 2)
    lin("gn", 0, 1)
    lin("qg", 1, 2, before_evac=tgroup("qn", 2, c=0))
    plan.extend(tgroup("qn", 2, c=1))
    for tt in range(TT):
        add("cs", tt=tt)
        plan.append(dict(kind="tp", stage="pc", g=0, c=tt, tt=tt))
        add("co_", tt=tt)
    att = [dict(b=b, h=h, tt=tt) for h in range(NQ) for tt in range(TT) for b in ("sel", "win")]
    for step in attention(att, 1)[0]:
        plan.extend(step)
    plan.extend(tgroup("on", 4))
    for c in range(2):
        lin("wo", c, 2)
    norm(8, True)
    ffn(4, "f4", 8, last=True)
    full, s = [], 0

    def split(upto):
        nonlocal s
        while s <= upto and s < len(units):
            full.append(dict(kind="split", unit=s))
            s += 1

    for item in plan:
        if item["kind"] == "lin" and item["unit"] == 0:
            split(RING - 1)
        full.append(item)
        if item["kind"] == "lin":
            split(item["unit"] + RING)
        if item["kind"] == "glu":
            split(item["unit"] + 1 + RING)
        if item["kind"] == "ffn":
            n = 3 * NJ
            item["have"] = s
            s = min(item["unit"] + n + RING, len(units))
    count = {}

    def number(key, n=1):
        count[key] = count.get(key, 0) + n
        return count[key] - n

    raw = []
    unit_raw, pair_after = {}, {}
    for item in full:
        k = item["kind"]
        item["n"] = number("kind " + k)
        if k == "split":
            unit_raw[item["unit"]] = len(raw)
            raw.append(("unit", item["unit"]))
        if k == "mod":
            item["raw"] = len(raw)
            raw.append(("mod", item["m"], item["half"]))
        if k == "lin" and item["part"] == 0:
            item["pi"] = number("pi")
            item["pair_before"] = count.get(f"pair{item['pi'] % 2}", 0)
        elif k in ("lin", "evac"):
            item["pi"] = count["pi"] - 1
        if k == "evac":
            st = item["stage"]
            if st not in ("out1", "co", "wo"):
                pair_after[item["pi"]] = number(f"pair{item['pi'] % 2}") + 1
            if st in ("qi", "qb", "kb", "qa", "ka"):
                item["rope"] = number("rope")
            if st in ("qb", "kb", "qa", "ka", "qg") or (st == "kv" and item["chunk"]):
                item["nq"] = number("nq")
        if k == "cmp" and item["s"] == 0:
            item["nq"] = number("nq")
        if k == "tp":
            item["tg"] = number("tg")
            if item["stage"] in PAIRED:
                item["hl"] = number("hl")
        if k == "ffn":
            item["tg"], item["hl"], item["gi"] = number("tg", NJ), number("hl", NJ), number("gi", NJ)
            for u in range(item["have"], min(item["unit"] + 3 * NJ + RING, len(units))):
                unit_raw[u] = len(raw)
                raw.append(("unit", u))
        if k == "glu":
            item["tg"], item["gi"] = number("tg"), number("gi")
        if k in ("ffn", "glu"):
            item["pairs_before"] = [count.get(f"pair{q}", 0) for q in range(2)]
        if k in ("qk", "sm", "pv") or (k == "tp" and item["stage"] == "p"):
            item["it"] = number("it " + k)
    find, made = {}, {}
    for item in full:
        k, st = item["kind"], item.get("stage")
        if k == "tp":
            key = item["it"] if st == "p" else (item["c"], item["g"]) if "c" in item else item["g"]
            find["tg", st, key] = item["tg"]
            if st in ("norm", "normf", "o", "merged", "on", "cb"):
                made = dict(made, **{str(2 * item["g"] + q): item["tg"] for q in range(2)})
        if k == "lin":
            find["pi", st, item["chunk"]] = item["pi"]
            find["unit", st, item["chunk"]] = item["unit"]
        if k == "glu":
            find["glu tg"] = item["tg"]
        if k == "mod":
            find["raw", item["m"]] = item["raw"]
        if k in ("lin", "ffn", "glu"):
            item["need"] = made
    return full, units, raw, unit_raw, find, pair_after


PAIRED = ("norm", "normf", "o", "merged", "on")


def two_block_program(nc, A, out):
    plan, units, raws, unit_raw, find, pair_after = make_plan()

    def rows(w):
        return w.rearrange("(k p) n -> p k n", p=P)

    w_mod, w_in = rows(A["w_mod"][0]), rows(A["w_in"][0])
    gate_up = [rows(A["w_gate_up"][0])] + [rows(A["ffn_w_gate_up_2"][l, i]) for l in range(2) for i in range(2)]
    down = [rows(A["w_down"][0])] + [rows(A["ffn_w_down_2"][l, i]) for l in range(2) for i in range(2)]
    in_at = dict(qa=0, ka=512, va=1024, qi=1536, ki=2048, qb=2120, kb=2632, vb=3144, ga=3656, gb=4680)
    plain = dict(ba=A["w_br_dsa"][0], bb=A["w_br_moba"][0], out1=A["w_out"][0], co=A["conv_w_out_2"][0],
                 kv=A["kv_w_2"], wo=A["nsa_w_o_2"][0])

    def unit_source(u):
        stage, c, part = units[u]
        ks = slice(4 * part, 4 * part + 4)
        if stage in in_at:
            if stage == "ki":
                return w_in[:, :, in_at["ki"]:in_at["ki"] + ID + IH], KT * (ID + IH)
            at = in_at[stage] + 512 * c
            return w_in[:, ks, at:at + 512], UNIT
        if stage in plain:
            return rows(plain[stage])[:, ks, 512 * c:512 * c + 512], UNIT
        if stage == "cb":
            return rows(A["conv_w_in_2"][0])[:, ks, 512 * c:512 * c + 512], UNIT
        if stage == "cv":
            v = rows(A["conv_w_in_2"][0])[:, ks, D:3 * D].rearrange("p k (s n) -> p k s n", s=2)
            return v[:, :, :, GC * c:GC * c + GC], UNIT
        if stage == "qg":
            return rows(A["nsa_w_qg_2"][0])[:, ks, 512 * c:512 * c + 512], UNIT
        if stage == "gn":
            return rows(A["nsa_w_qg_2"][0])[:, :, D:D + 48], KT * 48
        if stage == "cm":
            return rows(A["cmp_w1_2"][c])[:, 8 * part:8 * part + 8, :], UNIT
        f = int(stage[1])
        if stage.endswith("_d"):
            return down[f][:, 2 * c:2 * c + 2, :], UNIT
        return gate_up[f][:, ks, :].rearrange("p k (s n) -> p k s n", s=2)[:, :, :, GC * c:GC * c + GC], UNIT

    with ExitStack() as ctx:
        def sb(name, shape, dt=F32):
            return ctx.enter_context(nc.sbuf_tensor(name, [P, *shape], dt))

        sems = {}

        def sem(name):
            if name not in sems:
                sems[name] = ctx.enter_context(nc.semaphore(name))
            return sems[name]

        raw = sb("raw_ring", [RING, UNIT])
        w_hi = sb("w_hi_ring", [RING, UNIT], F32R)
        w_lo = sb("w_lo_ring", [RING, UNIT], F32R)
        h_hi = sb("h_hi", [KT, T], F32R)
        h_lo = sb("h_lo", [KT, T], F32R)
        f_hi = sb("f_hi", [2, 2, T], F32R)
        f_lo = sb("f_lo", [2, 2, T], F32R)
        xp_hi = sb("xp_hi", [16, 60], F32R)
        xp_lo = sb("xp_lo", [16, 60], F32R)
        x = sb("x", [TT, D])
        const = sb("const", [C_END])
        glu_s = sb("glu_s", [TT, GC])
        glu_a = sb("glu_a", [TT, GC])
        junk = sb("junk", [D])
        rows1 = sb("rows1", [P])
        rows2 = sb("rows2", [P])
        cols1 = sb("cols1", [P])
        cols2 = sb("cols2", [56])
        c_act = sb("c_act", [KT])
        modc = sb("modc", [2, 16])
        mod_s = sb("mod_s", [2, KT])
        ss = sb("ss", [TT])
        rstd = sb("rstd", [TT])
        qss = sb("qss", [TT, 8])
        qr = sb("qr", [TT, 8])
        half = sb("half", [16])
        rq = sb("rq", [2, TT, NH])
        rqn = sb("rqn", [TT, NQ])
        mn = sb("mn", [80])
        sm = sb("sm", [80])
        rc = sb("rc", [80])
        top8 = sb("top8", [8])
        arena_size = (nc.sbuf_bytes_remaining() if callable(nc.sbuf_bytes_remaining) else nc.sbuf_bytes_remaining) // 4 - 64
        arena = sb("arena", [arena_size])
        used = [0]

        def carve(*shape):
            n = int(np.prod(shape))
            v = arena[:, used[0]:used[0] + n]
            used[0] += n
            assert used[0] <= arena_size, (used[0], arena_size)
            if len(shape) == 1:
                return v
            names = "abcd"[:len(shape)]
            return v.rearrange(f"p ({' '.join(names)}) -> p {' '.join(names)}",
                               **{k: s for k, s in zip(names[1:], shape[1:])})

        s_s = carve(2, T)
        p_s = carve(2, T)
        pt_s = carve(2, T)
        base = used[0]
        gains = carve(4, HD)
        tab_c, tab_s = carve(TT, HD), carve(TT, HD)
        q_t, k_t = carve(NH, T), carve(NH, T)
        v_s = carve(TT, 512)
        qi_t = carve(4, T)
        ki_t = carve(T)
        o1 = carve(TT, D)
        sig = carve(TT, 2, D)
        gt = carve(2, D)
        b_row = arena[:, 0:D]
        acc = carve(2, 512)
        pq = carve(TT, 512)
        ro = carve(TT, 512)
        kiw = carve(TT, 72)
        kid = carve(TT, P)
        wi = carve(TT, IH)
        score = carve(TT, T)
        mask_d = carve(TT, T)
        rl = carve(2, T)
        hf = pq
        rope_a, rope_b = glu_s[:, :, :].rearrange("p a b -> p (a b)"), glu_a[:, :, :].rearrange("p a b -> p (a b)")
        used[0] = base
        v_t = carve(KT, 2 + T)
        cv_t = carve(KT, T)
        y_t = carve(KT, T)
        b_s = carve(TT, D)
        used[0] = base
        kv_d_flat = carve(2048)
        kv_d = kv_d_flat.rearrange("p (t s g u d) -> p t s g u d", t=TT, s=2, g=NG, u=2)
        x2 = carve(2, NG, T)
        kg = carve(3, DH)
        kgb = carve(4, DH)
        kn_t = carve(2, NG, T)
        vn_s = carve(2, TT, 256)
        kd = carve(TT, NG, 2, DH)
        kp = carve(TT, 256)
        xpf = carve(16, 60)
        w2 = carve(2, 2, DH)
        b1r = carve(2, 256)
        hc = carve(256)
        hc_t = carve(2, 60)
        hc_p = carve(2, NG, 4, 32)
        kc = carve(2, DH)
        kc_t = carve(60)
        v_bd = carve(NG, 256)
        gn = carve(TT, 48)
        q_n = carve(8, T)
        pqn = kv_d_flat[:, 0:1024].rearrange("p (t n) -> p t n", t=TT)
        o2 = carve(TT, D)
        pc_s = carve(16, 16)
        pc = carve(NQ, 32)
        pc_t = kp.rearrange("p a b -> p (a b)").rearrange("p (g q) -> p g q", g=NG)
        small = carve(64)

        ident = const[:, C_ID:C_ID + P]
        ones = const[:, C_ONE:C_ONE + P]

        bank = [ctx.enter_context(nc.psum_tensor(f"bank{b}", [P, 512], F32)) for b in range(8)]

        def mask_of(item):
            if item["b"] == "dsa":
                return mask_d[:, item["tt"], 0:P * (item["tt"] + 1)]
            return const[:, C_MASK + P * (1 - item["tt"]):C_MASK + 2 * P]

        def wait_group(eng, tg):
            eng.wait_ge(sem(f"t_free{tg % 2}"), tg // 2 + 1)

        def wait_bank(eng, tg):
            if tg >= 2:
                eng.wait_ge(sem(f"t_free{tg % 2}"), tg // 2)

        def wait_pair(eng, pi):
            eng.wait_ge(sem(f"pair_free{pi % 2}"), pair_after[pi])

        def wait_product(eng, stage, chunk):
            eng.wait_ge(sem("unit_used"), find["unit", stage, chunk] + 1)

        xu = {}
        for n, u in enumerate((0, 1, 2, 3, 4, 5, 5, 6, 7)):
            xu[n] = u

        def unit_view(ring, u, shape):
            v = ring[:, u % RING, 0:int(np.prod(shape))]
            names = "abc"[:len(shape)]
            return v.rearrange(f"p ({' '.join(names)}) -> p {' '.join(names)}",
                               **{k: s for k, s in zip(names[1:], shape[1:])})

        def unit_size(u):
            return unit_source(u)[1]

        class Tick:

            def __init__(self, eng, name):
                self.eng, self.sem, self.count = eng, sem(name), 0

            def __call__(self, ins):
                ins.then_inc(self.sem, 1)
                self.count += 1
                return self.count

            def wait(self, n=None):
                self.eng.wait_ge(self.sem, self.count if n is None else n)

            def step(self, ins):
                self(ins)
                self.wait()

        def ffn_loop(item):
            return (3, 3 if item["last"] else 4)

        block = ctx.enter_context(nc.Block())

        @block.sync
        def _(sp):
            def fill(slot, words, src):
                v, full = raw[:, slot, 0:words], sem(f"raw_full{slot}")
                if len(src.shape) == 3:
                    sp.dma_start(v.rearrange("p (k n) -> p k n", k=src.shape[1]), src).then_inc(full, 32)
                    return
                v = v.rearrange("p (k s n) -> p k s n", k=src.shape[1], s=2)
                for half_ in range(2):
                    sp.dma_start(v[:, :, half_, :], src[:, :, half_, :]).then_inc(full, 16)

            loops = {}
            for item in plan:
                if item["kind"] == "ffn":
                    first, turns = 3, 3
                    u0 = item["unit"] + 2 + 3 * (first - 1) + RING
                    loops[unit_raw[u0]] = (item, first, turns)
            r = 0
            while r < len(raws):
                if r in loops:
                    item, first, turns = loops[r]
                    f = item["f"]
                    gu = gate_up[f].rearrange("p k (s n) -> p k s n", s=2)
                    with sp.Fori(0, turns) as i:
                        for h in range(2):
                            for q in range(3):
                                rr = r + 3 * h + q
                                sp.wait_ge(sem("raw_done"), rr - RING + 1 + i * 6)
                                slot = rr % RING
                                if q < 2:
                                    at = (i * 2 + (first + 1 + h)) * GC
                                    src = gu[:, 4 * q:4 * q + 4, :, bass.ds(at, GC)]
                                else:
                                    src = down[f][:, bass.ds((i * 2 + (first + h)) * 2, 2), :]
                                fill(slot, UNIT, src)
                    r += 6 * turns
                    continue
                if r >= RING:
                    sp.wait_ge(sem("raw_done"), r - RING + 1)
                if raws[r][0] == "mod":
                    _, m, hf_ = raws[r]
                    src, words = w_mod[:, 4 * hf_:4 * hf_ + 4, 512 * m:512 * m + 512], UNIT
                else:
                    src, words = unit_source(raws[r][1])
                fill(r % RING, words, src)
                r += 1
            for tt in range(TT):
                sp.wait_ge(sem("x_ready"), 4 * 8)
                sp.dma_start(out.rearrange("(t p) d -> p t d", p=P)[:, tt, :], x[:, tt, :]).then_inc(sem("stored"), 16)
            sp.wait_ge(sem("stored"), 16 * TT)

        @block.gpsimd
        def _(pool):
            tick = Tick(pool, "pool_tick")

            def inverse_root(dst, src, width, scale, done):
                tick.step(pool.tensor_scalar(src, src, 1.0 / width, EPS, ALU.mult, ALU.add))
                n = dst.free_size() if callable(dst.free_size) else dst.free_size
                hv = half[0:dst.shape[0], 0:n]
                if len(dst.shape) == 3:
                    hv = hv.rearrange("p (a b) -> p a b", a=dst.shape[1])
                ins = pool.tensor_tensor(dst, src, hv, ALU.pow)
                if scale != 1.0:
                    tick.step(ins)
                    ins = pool.tensor_scalar(dst, dst, scale, None, ALU.mult)
                ins.then_inc(sem(done), 1)

            tick.step(pool.memset(half[:, :], -0.5))
            for item in plan:
                k = item["kind"]
                if k == "square":
                    pool.wait_ge(sem("ss_ready"), item["n"] + 1)
                    inverse_root(rstd[:, :], ss[:, :], D, 1.0, "rstd_ready")
                if k == "evac" and item["stage"] in ("qb", "kb", "qa", "ka"):
                    pool.wait_ge(sem("qss_ready"), item["nq"] + 1)
                    if item["stage"][0] == "q":
                        dst = rq[:, 0 if item["stage"] == "qa" else 1, :, :]
                        inverse_root(dst, qss[:, :, 0:NH], HD, -HD ** -0.5, "qr_ready")
                    else:
                        inverse_root(qr[:, :, 0:NH], qss[:, :, 0:NH], HD, 1.0, "qr_ready")
                if k == "evac" and item["stage"] == "kv" and item["chunk"]:
                    pool.wait_ge(sem("qss_ready"), item["nq"] + 1)
                    inverse_root(qr[:, :, 0:NG], qss[:, :, 0:NG], DH, 1.0, "qr_ready")
                if k == "evac" and item["stage"] == "qg":
                    pool.wait_ge(sem("qss_ready"), item["nq"] + 1)
                    c = item["chunk"]
                    inverse_root(rqn[:, :, 8 * c:8 * c + 8], qss[:, :, :], DH, -DH ** -0.5, "qr_ready")
                if k == "cmp" and item["s"] == 0:
                    pool.wait_ge(sem("qss_ready"), item["nq"] + 1)
                    inverse_root(qr[0:60, 0, 0:1], qss[0:60, 0, 0:1], DH, 1.0, "qr_ready")
                if k == "lin" and item["stage"] == "kv" and item["chunk"] == 0 and item["part"] == 0:
                    pool.wait_ge(sem("x_ready"), 4 * xu[5])
                    pool.dma_start(kgb[:, 0:3, :], A["k_norm_2"].rearrange("(o a) b -> o a b", o=1).to_broadcast([P, 3, DH])).then_inc(sem("small_full"), 16)
                    pool.dma_start(kgb[:, 3, :], A["q_norm_2"].to_broadcast([P, DH])).then_inc(sem("small_full"), 16)
                    pool.dma_start(w2, A["cmp_w2_2"].rearrange("s (k p) d -> p s k d", p=P)).then_inc(sem("small_full"), 16)
                    pool.dma_start(b1r[0:1], A["cmp_b1_2"].rearrange("(o s) n -> o s n", o=1)).then_inc(sem("small_full"), 16)
                    pool.memset(v_bd, 0.0)
                    pool.memset(pc, 0.0)
                    pool.memset(hc_p, 0.0).then_inc(sem("zeros_ready"), 1)

        @block.scalar
        def _(act):
            tick = Tick(act, "act_tick")
            act.dma_start(const[:, :], A["const"]).then_inc(sem("const_full"), 16)
            r1 = [A["g_mix_norm"], A["g_ffn_norm"], A["ffn_norm_2"], A["mix_norm_2"], A["kv_norm_2"], A["conv_w_2"], A["cmp_pos_2"]]
            at = 0
            for a in r1:
                n = int(np.prod(a.shape)) // P
                flat = a if len(a.shape) == 1 else (a.rearrange("a b -> (a b)") if len(a.shape) == 2 else a.rearrange("a b c -> (a b c)"))
                act.dma_start(rows1[at:at + n, :], flat.rearrange("(r q) -> r q", q=P)).then_inc(sem("rows_full"), 16)
                at += n
            assert at == P
            act.dma_start(rows2[0:8, :], A["c"].rearrange("a (r q) -> (a r) q", q=P)).then_inc(sem("rows_full"), 16)
            act.dma_start(rows2[8:56, :], A["b_mod"].rearrange("a (r q) -> (a r) q", q=P)).then_inc(sem("rows_full"), 16)
            for i, g in enumerate(("g_q_dsa", "g_k_dsa", "g_q_moba", "g_k_moba")):
                act.dma_start(gains[:, i, :], A[g].to_broadcast([P, HD])).then_inc(sem("gains_full"), 16)
            act.dma_start(b_row[0:1, :], A["b_mod"][0:1, 2 * D:3 * D]).then_inc(sem("b_row_full"), 16)
            act.dma_start(x[:, :, :], A["x"][0].rearrange("(t p) d -> p t d", p=P)).then_inc(sem("x_full"), 16)
            def split(u, r, gate):
                act.wait_ge(sem(f"raw_full{r % RING}"), 32 * (r // RING + 1))
                if gate is not None:
                    act.wait_ge(sem("unit_used"), gate)
                words = unit_size(u)
                act.activation(w_hi[:, u % RING, 0:words], raw[:, r % RING, 0:words], ACT.Copy)\
                   .then_inc(sem("hi_ready"), 1)

            for item in plan:
                k = item["kind"]
                if k == "init":
                    act.wait_ge(sem("init_done"), 1)
                    act.activation(c_act[:, :], bank[5][:, 0:KT], ACT.Silu).then_inc(sem("c_ready"), 1)
                if k == "split":
                    u = item["unit"]
                    split(u, unit_raw[u], u - RING + 1 if u >= RING else None)
                if k == "square":
                    n = item["n"]
                    if n == 0:
                        act.wait_ge(sem("x_full"), 16)
                    else:
                        act.wait_ge(sem("x_ready"), 4 * xu[n])
                        act.wait_ge(sem("rstd_ready"), n)
                    for tt in range(TT):
                        ins = act.activation(junk[:, :], x[:, tt, :], ACT.Square, accum_out=ss[:, tt:tt + 1])
                        tick.step(ins) if tt < TT - 1 else ins.then_inc(sem("ss_ready"), 1)
                if k == "tp":
                    st, tg, g = item["stage"], item["tg"], item["g"]
                    b = bank[6 + tg % 2]
                    if st in PAIRED or st in ("qi", "qb", "kb", "qa", "ka", "ki", "kvt", "qn", "hc", "kc", "pc") or \
                            (st == "p" and item["it"] % 2 == 0):
                        act.wait_ge(sem("t_done"), tg + 1)
                    free = sem(f"t_free{tg % 2}")
                    if st == "norm":
                        col = {2: 16, 3: 48, 4: 24, 5: 64, 6: 32, 7: 56, 8: 40}[item["norm"]]
                        for kk in range(2):
                            ins = act.activation(h_hi[:, 2 * g + kk, :], b[:, kk * T:(kk + 1) * T], ACT.Copy,
                                                 scale=cols1[:, col + 2 * g + kk:col + 2 * g + kk + 1])
                        ins.then_inc(sem("hi_t"), 1)
                    elif st == "normf":
                        n = item["norm"]
                        if g == 0:
                            act.wait_ge(sem("mod_ready"), n + 1)
                        for kk in range(2):
                            c = 2 * g + kk
                            ins = act.activation(hf[:, kk, T * (g % 2):T * (g % 2) + T], b[:, kk * T:(kk + 1) * T], ACT.Identity,
                                                 scale=mod_s[:, n, c:c + 1], bias=modc[:, n, c:c + 1])
                        ins.then_inc(sem("hi_t"), 1)
                    elif st in ("o", "merged", "on"):
                        kt = 2 * g
                        act.activation(h_hi[:, kt:kt + 2, :].rearrange("p a b -> p (a b)"), b[:, :], ACT.Copy)\
                           .then_inc(sem("hi_t"), 1)
                    elif st in ("qb", "kb", "qa", "ka"):
                        dst = (q_t if st[0] == "q" else k_t)[:, 2 * g:2 * g + 2, :].rearrange("p a b -> p (a b)")
                        act.activation(dst, b[:, :], ACT.Copy).then_inc(free, 1)
                    elif st == "qi":
                        act.activation(qi_t[:, 2 * g:2 * g + 2, :].rearrange("p a b -> p (a b)"), b[:, :], ACT.Copy)\
                           .then_inc(free, 1)
                    elif st == "ki":
                        act.activation(ki_t, b[:, 0:T], ACT.Copy).then_inc(free, 1)
                    elif st == "kvt" and item["c"] == 0:
                        s_, g0 = divmod(2 * g, NG)
                        bv = b[:, :].rearrange("p (a t) -> p a t", a=2)
                        act.activation(x2[0:64, s_, g0:g0 + 2, :], bv[0:64], ACT.Copy)
                        act.activation(x2[64:128, s_, g0:g0 + 2, 0:T - 1], bv[64:128, :, 1:T], ACT.Copy)\
                           .then_inc(free, 1)
                    elif st == "kvt":
                        act.activation(kn_t[:, item["c"] - 1, 2 * g:2 * g + 2, :].rearrange("p a b -> p (a b)"),
                                       b[:, :], ACT.Copy).then_inc(free, 1)
                    elif st == "qn":
                        m = 4 * item["c"] + 2 * g
                        act.activation(q_n[:, m:m + 2, :].rearrange("p a b -> p (a b)"), b[:, :], ACT.Copy)\
                           .then_inc(free, 1)
                    elif st == "hc":
                        act.wait_ge(sem("zeros_ready"), 1)
                        bv = b[:, 0:120].rearrange("p (k c) -> p k c", k=2)
                        if item["c"] == 0:
                            act.activation(hc_t, bv, ACT.Copy).then_inc(free, 1)
                        else:
                            for kk in range(2):
                                for hh in range(4):
                                    ins = act.activation(hc_p[:, kk, :, hh, 0:NC],
                                                         bv[:, kk, :].rearrange("p (g n) -> p g n", g=NG), ACT.Copy)
                            ins.then_inc(free, 1)
                    elif st == "kc":
                        act.activation(kc_t, b[:, 0:60], ACT.Copy).then_inc(free, 1)
                    elif st == "pc":
                        act.activation(pc_t.rearrange("p a b -> p (a b)"), b[:, :], ACT.Copy).then_inc(free, 1)
                    elif st == "p" and item["it"] % 2 == 0:
                        n = P * (item["tt"] + 1)
                        act.activation(pt_s[:, item["it"] % 2, 0:n], b[:, 0:n], ACT.Copy).then_inc(free, 1)
                if k == "evac":
                    st, c, pi = item["stage"], item["chunk"], item["pi"]
                    b = [bank[2 * (pi % 2) + tt] for tt in range(TT)]
                    free = sem(f"pair_free{pi % 2}")
                    if st not in ("ba", "bb", "out1", "co", "wo"):
                        wait_product(act, st, c)
                    if st in ("qi", "qb", "kb", "qa", "ka"):
                        if item["rope"]:
                            act.wait_ge(sem("rope_done"), item["rope"])
                        for tt in range(TT):
                            ins = act.activation(pq[:, tt, :], b[tt][:, :], ACT.Copy)
                        if st != "qi":
                            for tt in range(TT):
                                ins = act.activation(junk[:, tt * 512:(tt + 1) * 512], b[tt][:, :], ACT.Square)
                        ins.then_inc(free, 1)
                    elif st == "ki":
                        for tt in range(TT):
                            ins = act.activation(kiw[:, tt, :], b[tt][:, 0:72], ACT.Copy)
                        ins.then_inc(free, 1)
                    elif st in ("va", "vb"):
                        if st == "va":
                            act.wait_ge(sem("pv_done"), 8)
                        for tt in range(TT):
                            ins = act.activation(v_s[:, tt, :], b[tt][:, :], ACT.Copy)
                        ins.then_inc(free, 1)
                    elif st in ("ga", "gb"):
                        for tt in range(TT):
                            ins = act.activation(sig[:, tt, 0 if st == "ga" else 1, 512 * c:512 * c + 512], b[tt][:, :], ACT.Copy)
                        ins.then_inc(free, 1)
                    elif st == "cb":
                        for tt in range(TT):
                            ins = act.activation(b_s[:, tt, 512 * c:512 * c + 512], b[tt][:, :], ACT.Copy, scale=rstd[:, tt:tt + 1])
                        ins.then_inc(free, 1)
                    elif st == "kv" and c == 0:
                        act.wait_ge(sem("rstd_ready"), 6)
                        for tt in range(TT):
                            for s_ in range(2):
                                for dup in range(2):
                                    ins = act.activation(kv_d[:, tt, s_, :, dup, :],
                                                         b[tt][:, 256 * s_:256 * s_ + 256].rearrange("p (g d) -> p g d", g=NG),
                                                         ACT.Copy, scale=rstd[:, tt:tt + 1])
                        ins.then_inc(free, 1)
                    elif st == "kv":
                        if c == 2:
                            act.wait_ge(sem("kd_done"), 1)
                        for tt in range(TT):
                            act.activation(kp[:, tt, :], b[tt][:, 0:256], ACT.Copy, scale=rstd[:, tt:tt + 1])
                            act.activation(junk[:, tt * 256:(tt + 1) * 256], b[tt][:, 0:256], ACT.Square, scale=rstd[:, tt:tt + 1])
                            ins = act.activation(vn_s[:, c - 1, tt, :], b[tt][:, 256:512], ACT.Copy, scale=rstd[:, tt:tt + 1])
                        ins.then_inc(free, 1)
                    elif st == "cm":
                        act.activation(hc[0:60], b[0][0:60, 0:256], ACT.Gelu_apprx_tanh).then_inc(free, 1)
                    elif st == "gn":
                        act.wait_ge(sem("rstd_ready"), 8)
                        for tt in range(TT):
                            ins = act.activation(gn[:, tt, :], b[tt][:, 0:48], ACT.Sigmoid, scale=rstd[:, tt:tt + 1])
                        ins.then_inc(free, 1)
                    elif st == "qg":
                        act.wait_ge(sem("rstd_ready"), 8)
                        if c:
                            act.wait_ge(sem("qss_ready"), item["nq"])
                            act.wait_ge(sem("t_done"), find["tg", "qn", (0, 1)] + 1)
                        for tt in range(TT):
                            act.activation(pqn[:, tt, :], b[tt][:, :], ACT.Copy, scale=rstd[:, tt:tt + 1])
                            ins = act.activation(junk[:, tt * 512:(tt + 1) * 512], b[tt][:, :], ACT.Square, scale=rstd[:, tt:tt + 1])
                        ins.then_inc(free, 1)
                if k == "ix":
                    act.wait_ge(sem("ix_done"), item["n"] + 1)
                    for hh in range(2):
                        n = P * (item["tt"] + 1)
                        if item["n"]:
                            act.wait_ge(sem("ix_used"), 2 * item["n"] - 1 + hh)
                        act.activation(rl[:, hh, 0:n], bank[4 + hh][:, 0:n], ACT.Relu).then_inc(sem("rl_ready"), 1)
                if k == "sm":
                    it = item["it"]
                    n = P * (item["tt"] + 1)
                    act.wait_ge(sem("sm_done"), it + 1)
                    if it >= 2:
                        act.wait_ge(sem("t_done"), find["tg", "p", it - 2] + 1)
                    act.activation(p_s[:, it % 2, 0:n], s_s[:, it % 2, 0:n], ACT.Exp, scale=-1.0,
                                   bias=mn[:, it:it + 1], accum_out=sm[:, it:it + 1]).then_inc(sem("exp_done"), 1)
                if k == "sigmoid":
                    act.wait_ge(sem("o_ready"), 2 * NH * TT)
                    act.dma_start(b_row[0:1, :], A["b_mod"][0:1, 5 * D:6 * D]).then_inc(sem("b_row_full"), 16)
                    for c_ in range(2):
                        wait_pair(act, find["pi", "gb", c_])
                    for tt in range(TT):
                        for a in range(2):
                            ins = act.activation(sig[:, tt, a, :], sig[:, tt, a, :], ACT.Sigmoid)
                    ins.then_inc(sem("sig_ready"), 1)
                if k == "cs":
                    act.wait_ge(sem("cs_ready"), item["tt"] + 1)
                    act.activation(pc_s, pc_s, ACT.Exp, scale=-1.0).then_inc(sem("cs_exp"), 1)
                if k == "co_":
                    act.wait_ge(sem("cv_done"), item["tt"] + 1)
                    for a in range(2):
                        ins = act.activation(o2[:, item["tt"], 512 * a:512 * a + 512], bank[4 + a][:, :], ACT.Copy)
                    ins.then_inc(sem("oc_ready"), 1)
                if k == "xp":
                    act.wait_ge(sem("xp_full"), item["s"] + 1)
                    act.activation(xp_hi[:, :, :].rearrange("p a b -> p (a b)"), xpf.rearrange("p a b -> p (a b)"),
                                   ACT.Copy).then_inc(sem("xp_hi_ready"), 1)
                if k == "glu":
                    if item["j"] == 0:
                        act.wait_ge(sem("rstd_ready"), 4)
                    act.wait_ge(sem("unit_used"), item["unit"] + 2)
                    for tt in range(TT):
                        act.activation(glu_s[:, tt, :], bank[tt][:, 0:GC], ACT.Copy, scale=rstd[:, tt:tt + 1])\
                           .then_inc(sem("sg_ready"), 1)
                    act.wait_ge(sem("t_done"), item["tg"] + 1)
                    act.activation(v_t[:, 2 * item["j"]:2 * item["j"] + 2, 2:2 + T],
                                   bank[6 + item["tg"] % 2][:, :].rearrange("p (a t) -> p a t", a=2), ACT.Copy)\
                       .then_inc(sem(f"t_free{item['tg'] % 2}"), 1)
                if k == "ffn":
                    f = item["f"]
                    if f:
                        act.wait_ge(sem("rstd_ready"), item["norm"] + 1)

                    def step(jb, i=None):
                        two = lambda a: 0 if i is None else a * 2 * i

                        def next_split(q):
                            u = item["unit"] + (2 + 3 * (jb - 1) if jb else 0) + q + RING
                            if u >= len(units) or u < item["have"]:
                                return
                            split_at(u)

                        def split_at(u):
                            act.wait_ge(sem(f"raw_full{unit_raw[u] % RING}"), 32 * (unit_raw[u] // RING + 1) + two(32))
                            act.wait_ge(sem("unit_used"), u - RING + 1 + two(3))
                            act.activation(w_hi[:, u % RING, :], raw[:, unit_raw[u] % RING, :], ACT.Copy)\
                               .then_inc(sem("hi_ready"), 1)

                        qs = [0, 1, 2] if jb else [0, 1]
                        if jb < NJ:
                            next_split(0)
                            act.wait_ge(sem("unit_used"), item["unit"] + 3 * jb + (1 if jb else 2) + two(3))
                            for tt in range(TT):
                                act.activation(glu_s[:, tt, :], bank[tt][:, 0:GC], ACT.Silu,
                                               scale=rstd[:, tt:tt + 1] if f else 1.0).then_inc(sem("sg_ready"), 1)
                            for q in qs[1:]:
                                next_split(q)
                            tg = item["tg"] + jb
                            act.wait_ge(sem("t_done"), tg + 1 + two(1))
                            act.activation(f_hi[:, jb % 2, :, :].rearrange("p a b -> p (a b)"), bank[6 + tg % 2][:, :],
                                           ACT.Copy).then_inc(sem("hi_t"), 1)
                        else:
                            u = item["unit"] + 3 * NJ - 1 + RING
                            if u < len(units):
                                split_at(u)

                    first, turns = ffn_loop(item)
                    for j in range(first):
                        step(j)
                    with act.Fori(0, turns) as i:
                        for h in range(2):
                            step(first + h, i)
                    for j in range(first + 2 * turns, NJ + 1):
                        step(j)

        @block.vector
        def _(dve):
            tick = Tick(dve, "dve_tick")

            updates = [0]

            def lo_split(u, r, two=lambda a: 0):
                dve.wait_ge(sem("hi_ready"), u + 1 + two(3))
                words = unit_size(u)
                dve.tensor_tensor(w_lo[:, u % RING, 0:words], raw[:, r % RING, 0:words],
                                  w_hi[:, u % RING, 0:words].bitcast(F32), ALU.subtract).then_inc(sem("raw_done"), 1)

            def rope(dst, src, cos, sin, heads, w, done=None):
                n = heads * w
                s3 = src.rearrange("p (h w) -> p h w", h=heads)
                a3 = rope_a[:, 0:n].rearrange("p (h w) -> p h w", h=heads)
                b3 = rope_b[:, 0:n].rearrange("p (h w) -> p h w", h=heads)

                def over(t):
                    return t.unsqueeze(1).to_broadcast([P, heads, t.shape[-1]])

                tick(dve.tensor_tensor(a3, s3, over(cos), ALU.mult))
                tick(dve.tensor_tensor(b3[:, :, 0:w // 2], s3[:, :, w // 2:w], over(sin[:, 0:w // 2]), ALU.mult))
                tick.step(dve.tensor_tensor(b3[:, :, w // 2:w], s3[:, :, 0:w // 2], over(sin[:, w // 2:w]), ALU.mult))
                ins = dve.tensor_tensor(dst, rope_a[:, 0:n], rope_b[:, 0:n], ALU.add)
                tick.step(ins) if done is None else ins.then_inc(sem(done), 1)

            def update(tt, nb, src, how):
                xv = x[:, tt, 512 * nb:512 * nb + 512]
                if how == "half":
                    ins = dve.scalar_tensor_tensor(xv, src, 0.5, xv, ALU.mult, ALU.add)
                elif how == "one":
                    ins = dve.tensor_tensor(xv, src, xv, ALU.add)
                else:
                    g = gt[:, how, 512 * nb:512 * nb + 512]
                    tmp = rope_a if updates[0] % 2 else rope_b
                    if updates[0] >= 2:
                        dve.wait_ge(sem("x_ready"), updates[0] - 1)
                    tick.step(dve.tensor_tensor(tmp, src, g, ALU.mult))
                    ins = dve.tensor_tensor(xv, tmp, xv, ALU.add)
                ins.then_inc(sem("x_ready"), 1)
                updates[0] += 1

            for item in plan:
                k = item["kind"]
                if k == "init":
                    dve.wait_ge(sem("init_done"), 1)
                    tick(dve.tensor_copy(cols1[:, :], bank[6][:, 0:P]))
                    dve.tensor_copy(cols2[:, :], bank[7][:, 0:56]).then_inc(sem("cols_ready"), 1)
                if k == "split":
                    lo_split(item["unit"], unit_raw[item["unit"]])
                if k == "mod":
                    m, hh, r = item["m"], item["half"], item["raw"]
                    dve.wait_ge(sem(f"raw_full{r % RING}"), 32 * (r // RING + 1))
                    if item["n"] == 0:
                        dve.wait_ge(sem("c_ready"), 1)
                    if hh == 0 and m >= 2:
                        dve.wait_ge(sem("t_done"), find["tg", "mod", m - 2] + 1)
                    wv = raw[:, r % RING, :].rearrange("p (k n) -> p k n", k=4)
                    for kk in range(4):
                        kt = 4 * hh + kk
                        a = acc[:, m % 2, :]
                        if kt == 0:
                            ins = dve.tensor_scalar(a, wv[:, kk, :], c_act[:, 0:1], None, ALU.mult)
                        else:
                            ins = dve.scalar_tensor_tensor(a, wv[:, kk, :], c_act[:, kt:kt + 1], a, ALU.mult, ALU.add)
                        if kk < 3:
                            tick.step(ins)
                        else:
                            ins.then_inc(sem("raw_done"), 1)
                            if hh == 0:
                                dve.wait_ge(sem("raw_done"), r + 1)
                if k == "mod_a":
                    n = item["norm"]
                    for g in range(6 * n + 2 * n * 0, 6 * n + 4):
                        wait_group(dve, find["tg", "mod", g])
                    dve.scalar_tensor_tensor(mod_s[:, n, :], modc[:, n, 8:16], 1.0, cols1[:, 8 * n:8 * n + 8],
                                             ALU.add, ALU.mult).then_inc(sem("mod_ready"), 1)
                if k == "scale_x":
                    dve.wait_ge(sem("rstd_ready"), item["norm"] + 1)
                    for tt in range(TT):
                        ins = dve.tensor_scalar(o1[:, tt, :], x[:, tt, :], rstd[:, tt:tt + 1], None, ALU.mult)
                        ins.then_inc(sem("xn_ready"), 1)
                if k == "tp":
                    st, tg, g = item["stage"], item["tg"], item["g"]
                    b = bank[6 + tg % 2]
                    free = sem(f"t_free{tg % 2}")
                    if st == "mod":
                        dve.wait_ge(sem("t_done"), tg + 1)
                        which = g // 2
                        if which in (2, 5):
                            dve.tensor_copy(gt[:, which // 3, 512 * (g % 2):512 * (g % 2) + 512], b[:, :]).then_inc(free, 1)
                        else:
                            n, at = (0, which) if which < 2 else (1, which - 3)
                            at = 8 * at + 4 * (g % 2)
                            bc = 8 + 4 * g
                            dve.tensor_tensor(modc[:, n, at:at + 4], b[:, 0:4], cols2[:, bc:bc + 4], ALU.add).then_inc(free, 1)
                    if st in PAIRED:
                        dve.wait_ge(sem("hi_t"), item["hl"] + 1)
                        if st == "norm":
                            col = {2: 16, 3: 48, 4: 24, 5: 64, 6: 32, 7: 56, 8: 40}[item["norm"]]
                            for kk in range(2):
                                c = 2 * g + kk
                                ins = dve.scalar_tensor_tensor(h_lo[:, c, :], b[:, kk * T:(kk + 1) * T], cols1[:, col + c:col + c + 1],
                                                               h_hi[:, c, :].bitcast(F32), ALU.mult, ALU.subtract)
                            ins.then_inc(free, 1)
                        elif st == "normf":
                            hv = h_hi[:, 2 * g:2 * g + 2, :]
                            tick.step(dve.tensor_copy(hv, hf[:, :, T * (g % 2):T * (g % 2) + T]))
                            dve.tensor_tensor(h_lo[:, 2 * g:2 * g + 2, :], hf[:, :, T * (g % 2):T * (g % 2) + T], hv.bitcast(F32), ALU.subtract)\
                               .then_inc(free, 1)
                        else:
                            dve.tensor_tensor(h_lo[:, 2 * g:2 * g + 2, :].rearrange("p a b -> p (a b)"), b[:, :],
                                              h_hi[:, 2 * g:2 * g + 2, :].rearrange("p a b -> p (a b)").bitcast(F32), ALU.subtract)\
                               .then_inc(free, 1)
                    if st == "cb":
                        c0 = 2 * g
                        dve.wait_ge(sem("t_done"), tg + 1)
                        yv = y_t[:, c0:c0 + 2, :].rearrange("p a b -> p (a b)")
                        hv = h_hi[:, c0:c0 + 2, :].rearrange("p a b -> p (a b)")
                        tick.step(dve.tensor_tensor(yv, b[:, :], cv_t[:, c0:c0 + 2, :].rearrange("p a b -> p (a b)"), ALU.mult))
                        tick.step(dve.tensor_copy(hv, yv))
                        dve.tensor_tensor(h_lo[:, c0:c0 + 2, :].rearrange("p a b -> p (a b)"), yv, hv.bitcast(F32), ALU.subtract)\
                           .then_inc(free, 1)
                    if st == "p" and item["it"] % 2:
                        n = P * (item["tt"] + 1)
                        dve.wait_ge(sem("t_done"), tg + 1)
                        dve.tensor_copy(pt_s[:, item["it"] % 2, 0:n], b[:, 0:n]).then_inc(free, 1)
                if k == "conv":
                    wait_group(dve, find["glu tg"])
                    wait_group(dve, find["glu tg"] - 1)
                    dve.wait_ge(sem("v_t_ready"), 1)
                    for kt in range(KT):
                        cw = [cols1[:, 72 + 8 * w + kt:73 + 8 * w + kt] for w in range(3)]
                        cv = cv_t[:, kt, :]
                        tick.step(dve.tensor_scalar(cv, v_t[:, kt, 0:T], cw[0], None, ALU.mult))
                        tick.step(dve.scalar_tensor_tensor(cv, v_t[:, kt, 1:1 + T], cw[1], cv, ALU.mult, ALU.add))
                        tick.step(dve.scalar_tensor_tensor(cv, v_t[:, kt, 2:2 + T], cw[2], cv, ALU.mult, ALU.add))
                if k == "evac":
                    st, c, pi = item["stage"], item["chunk"], item["pi"]
                    b = [bank[2 * (pi % 2) + tt] for tt in range(TT)]
                    free = sem(f"pair_free{pi % 2}")
                    if st in ("ba", "bb"):
                        wait_product(dve, st, c)
                        dve.wait_ge(sem("sig_ready"), 1)
                        if st == "bb":
                            wait_pair(dve, find["pi", "ba", c])
                        for tt in range(TT):
                            a = 0 if st == "ba" else 1
                            v = sig[:, tt, a, 512 * c:512 * c + 512]
                            if st == "ba":
                                ins = dve.tensor_tensor(v, b[tt][:, :], v, ALU.mult)
                                ins.then_inc(free, 1) if tt else tick(ins)
                            else:
                                tick.step(dve.tensor_tensor(v, b[tt][:, :], v, ALU.mult))
                                ins = dve.tensor_tensor(sig[:, tt, 0, 512 * c:512 * c + 512],
                                                        sig[:, tt, 0, 512 * c:512 * c + 512], v, ALU.add)
                                ins.then_inc(free, 1) if tt else tick(ins)
                    elif st in ("out1", "co", "wo"):
                        wait_product(dve, st, c)
                        for tt in range(TT):
                            update(tt, c, b[tt][:, :], 0 if st == "out1" else "one")
                    elif st in ("qb", "kb", "qa", "ka"):
                        gi = ("qa", "ka", "qb", "kb").index(st)
                        if item["nq"] == 0:
                            dve.wait_ge(sem("gains_full"), 16 * 4)
                            dve.wait_ge(sem("const_full"), 16)
                        gv = gains[:, gi, :]
                        for tt in range(TT):
                            cb = const[:, C_COSH + tt * HD:C_COSH + (tt + 1) * HD]
                            sb_ = const[:, C_SINH + tt * HD:C_SINH + (tt + 1) * HD]
                            tick(dve.tensor_tensor(tab_c[:, tt, :], cb, gv, ALU.mult))
                            tick(dve.tensor_tensor(tab_s[:, tt, 0:64], sb_[:, 0:64], gv[:, 64:128], ALU.mult))
                            tick(dve.tensor_tensor(tab_s[:, tt, 64:128], sb_[:, 64:128], gv[:, 0:64], ALU.mult))
                        tick.wait()
                        wait_pair(dve, pi)
                        for tt in range(TT):
                            ins = dve.tensor_reduce(qss[:, tt, 0:NH], junk[:, tt * 512:(tt + 1) * 512].rearrange("p (h w) -> p h w", h=NH),
                                                    AX.X, ALU.add)
                            tick(ins) if tt == 0 else ins.then_inc(sem("qss_ready"), 1)
                        before = {"qb": "qi", "kb": "qb", "qa": "kb", "ka": "qa"}[st]
                        dve.wait_ge(sem("t_done"), find["tg", before, 1] + 1)
                        for tt in range(TT):
                            rope(ro[:, tt, :], pq[:, tt, :], tab_c[:, tt, :], tab_s[:, tt, :], NH, HD,
                                 "rope_done" if st[0] == "q" and tt else None)
                        dve.wait_ge(sem("qr_ready"), item["nq"] + 1)
                        if st[0] == "k":
                            for tt in range(TT):
                                rv = ro[:, tt, :].rearrange("p (h w) -> p h w", h=NH)
                                ins = dve.tensor_tensor(rv, rv, qr[:, tt, 0:NH].unsqueeze(2).to_broadcast([P, NH, HD]), ALU.mult)
                                ins.then_inc(sem("rope_done"), 1) if tt else tick(ins)
                    elif st == "qi":
                        wait_pair(dve, pi)
                        for tt in range(TT):
                            rope(ro[:, tt, :], pq[:, tt, :], const[:, C_COSI + tt * ID:C_COSI + (tt + 1) * ID],
                                 const[:, C_SINI + tt * ID:C_SINI + (tt + 1) * ID], IH, ID, "rope_done" if tt else None)
                    elif st == "ki":
                        wait_pair(dve, pi)
                        dve.wait_ge(sem("const_full"), 16)
                        for tt in range(TT):
                            tick.step(dve.tensor_scalar(wi[:, tt, :], kiw[:, tt, ID:ID + IH], HI_SCALE, None, ALU.mult))
                            rope(kid[:, tt, 0:ID], kiw[:, tt, 0:ID], const[:, C_COSI + tt * ID:C_COSI + (tt + 1) * ID],
                                 const[:, C_SINI + tt * ID:C_SINI + (tt + 1) * ID], 1, ID)
                            ins = dve.tensor_copy(kid[:, tt, ID:2 * ID], kid[:, tt, 0:ID])
                            ins.then_inc(sem("kid_ready"), 1) if tt else tick(ins)
                    elif st == "kv" and c:
                        wait_pair(dve, pi)
                        if c == 1:
                            dve.wait_ge(sem("small_full"), 16 * 4)
                            tick.step(dve.tensor_tensor(kg, kgb[:, 0:3, :], kgb[:, 3, :].unsqueeze(1).to_broadcast([P, 3, DH]), ALU.mult))
                        for tt in range(TT):
                            ins = dve.tensor_reduce(qss[:, tt, 0:NG], junk[:, tt * 256:(tt + 1) * 256].rearrange("p (h w) -> p h w", h=NG),
                                                    AX.X, ALU.add)
                            tick(ins) if tt == 0 else ins.then_inc(sem("qss_ready"), 1)
                        dve.wait_ge(sem("qr_ready"), item["nq"] + 1)
                        if c == 2:
                            dve.wait_ge(sem("t_done"), find["tg", "kvt", (1, 1)] + 1)
                        for tt in range(TT):
                            kv3 = kp[:, tt, :].rearrange("p (g w) -> p g w", g=NG)
                            tick.step(dve.tensor_tensor(kv3, kv3, qr[:, tt, 0:NG].unsqueeze(2).to_broadcast([P, NG, DH]), ALU.mult))
                            for dup in range(2):
                                ins = dve.tensor_tensor(kd[:, tt, :, dup, :], kv3, kg[:, c, :].unsqueeze(1).to_broadcast([P, NG, DH]), ALU.mult)
                                ins.then_inc(sem("kd_done"), 1) if tt and dup else tick(ins)
                    elif st == "qg":
                        wait_pair(dve, pi)
                        for tt in range(TT):
                            ins = dve.tensor_reduce(qss[:, tt, :], junk[:, tt * 512:(tt + 1) * 512].rearrange("p (h w) -> p h w", h=8),
                                                    AX.X, ALU.add)
                            tick(ins) if tt == 0 else ins.then_inc(sem("qss_ready"), 1)
                        dve.wait_ge(sem("qr_ready"), item["nq"] + 1)
                if k == "ix":
                    n = P * (item["tt"] + 1)
                    for hh in range(2):
                        h = 2 * item["pair"] + hh
                        sc = score[:, item["tt"], 0:n]
                        dve.wait_ge(sem("rl_ready"), 2 * item["n"] + hh + 1)
                        if h:
                            dve.wait_ge(sem("ix_used"), 2 * item["n"] + hh)
                        prev = const[:, C_MASK + P * (1 - item["tt"]):C_MASK + 2 * P] if h == 0 else sc
                        dve.scalar_tensor_tensor(sc, rl[:, hh, 0:n], wi[:, item["tt"], h:h + 1], prev, ALU.mult, ALU.add)\
                           .then_inc(sem("ix_used"), 1)
                if k == "topk":
                    tt = item["tt"]
                    n = P * (tt + 1)
                    sc = score[:, tt, 0:n]
                    dve.wait_ge(sem("ix_used"), 8 * (tt + 1))
                    for _ in range(TOPK // 8):
                        tick.step(dve.max(top8[:, :], sc))
                        tick.step(dve.match_replace(sc, top8[:, :], sc, TAKEN))
                    tick.step(dve.tensor_scalar(mask_d[:, tt, 0:n], sc, -2e38, NEG, ALU.is_gt, ALU.mult))
                    tick.step(dve.tensor_tensor(mask_d[:, tt, 0:n], mask_d[:, tt, 0:n],
                                                const[:, C_MASK + P * (1 - tt):C_MASK + 2 * P], ALU.add))
                if k == "sm":
                    it, tt = item["it"], item["tt"]
                    n = P * (tt + 1)
                    dve.wait_ge(sem("qk_done"), it + 1)
                    if it >= 2:
                        dve.wait_ge(sem("exp_done"), it - 1)
                    if item["b"] in ("dsa", "moba"):
                        scale = rq[:, 0 if item["b"] == "dsa" else 1, tt, item["h"]:item["h"] + 1]
                    else:
                        scale = rqn[:, tt, item["h"]:item["h"] + 1]
                    dve.tensor_tensor_reduce(s_s[:, it % 2, 0:n], bank[4 + it % 2][:, 0:n], mask_of(item), scale, 3e38,
                                             ALU.add, ALU.min, mn[:, it:it + 1]).then_inc(sem("sm_done"), 1)
                if k == "pv":
                    it, tt, h = item["it"], item["tt"], item["h"]
                    tick.step(dve.reciprocal(rc[:, it:it + 1], sm[:, it:it + 1]))
                    dve.wait_ge(sem("pv_done"), it + 1)
                    if item["b"] in ("dsa", "moba"):
                        at = 512 * (item["b"] == "moba") + HD * h
                        dve.tensor_scalar(o1[:, tt, at:at + HD], bank[6 + find["tg", "p", it] % 2][:, T:T + HD], rc[:, it:it + 1], None, ALU.mult)\
                           .then_inc(sem("o_ready"), 1)
                    else:
                        j = 1 + (item["b"] == "win")
                        if item["b"] == "sel" and it == 16:
                            dve.wait_ge(sem("oc_ready"), 2)
                        gcol = gn[:, tt, 3 * h + j:3 * h + j + 1]
                        tick.step(dve.tensor_tensor(rc[:, it:it + 1], rc[:, it:it + 1], gcol, ALU.mult))
                        ov = o2[:, tt, DH * h:DH * h + DH]
                        dve.scalar_tensor_tensor(ov, bank[6 + find["tg", "p", it] % 2][:, T:T + DH], rc[:, it:it + 1], ov, ALU.mult, ALU.add)\
                           .then_inc(sem("o_ready"), 1)
                if k == "cs":
                    tt = item["tt"]
                    dve.wait_ge(sem("cs_done"), tt + 1)
                    if tt:
                        dve.wait_ge(sem("t_done"), find["tg", "pc", (0, 0)] + 1)
                    pv = pc_s.rearrange("p (m e) n -> p m e n", e=2)
                    for e in range(2):
                        r_ = rqn[:, tt, :].rearrange("p (m e) -> p m e", e=2)[:, :, e].unsqueeze(2).to_broadcast([P, 8, NC])
                        src = bank[4 + e][:, 0:128].rearrange("p (m n) -> p m n", n=16)[:, :, 0:NC]
                        tick(dve.tensor_tensor(pv[:, :, e, 0:NC], src, r_, ALU.mult))
                    tick.wait()
                    v = pc_s[:, :, 0:NC]
                    cm = const[:, C_CM + 16 * tt:C_CM + 16 * tt + NC].unsqueeze(1).to_broadcast([P, NQ, NC])
                    cv = const[:, C_CV + 16 * tt:C_CV + 16 * tt + NC].unsqueeze(1).to_broadcast([P, NQ, NC])
                    tick.step(dve.tensor_tensor(v, v, cm, ALU.add))
                    tick.step(dve.tensor_reduce(small[:, 0:NQ], v, AX.X, ALU.min))
                    tick.step(dve.memset(pc_s[:, :, NC:16], 0.0))
                    dve.tensor_tensor(v, v, small[:, 0:NQ].unsqueeze(2).to_broadcast([P, NQ, NC]), ALU.subtract)\
                       .then_inc(sem("cs_ready"), 1)
                    dve.wait_ge(sem("cs_exp"), tt + 1)
                    tick.step(dve.tensor_reduce(small[:, 16:32], v, AX.X, ALU.add))
                    tick.step(dve.reciprocal(small[:, 32:48], small[:, 16:32]))
                    g0 = gn[:, tt, :].rearrange("p (h j) -> p h j", j=3)[:, :, 0]
                    tick.step(dve.tensor_tensor(small[:, 32:48], small[:, 32:48], g0, ALU.mult))
                    tick.step(dve.tensor_tensor(v, v, cv, ALU.mult))
                    if tt == 0:
                        dve.wait_ge(sem("zeros_ready"), 1)
                    dve.tensor_tensor(pc[:, :, 0:NC], v, small[:, 32:48].unsqueeze(2).to_broadcast([P, NQ, NC]), ALU.mult)\
                       .then_inc(sem("pc_ready"), 1)
                if k == "xp":
                    s_ = item["s"]
                    if s_ == 0:
                        wait_group(dve, find["tg", "kvt", (0, 2)])
                        wait_group(dve, find["tg", "kvt", (0, 3)])
                    else:
                        dve.wait_ge(sem("xp_hi_ready"), 1)
                        wait_product(dve, "cm", 0)
                    pos = cols1[:, 96 + 16 * s_:96 + 16 * s_ + 16]
                    for g in range(NG):
                        xv = x2[:, s_, g, :].rearrange("p (n a) -> p n a", a=CS)
                        for e in range(2):
                            dst = xpf[:, 8 * e:8 * e + 8, NC * g:NC * g + NC].rearrange("p k n -> p n k")
                            ins = dve.tensor_tensor(dst, xv[:, e:e + NC, 0:CS:2],
                                                    pos[:, 8 * e:8 * e + 8].unsqueeze(1).to_broadcast([P, NC, 8]), ALU.add)
                            ins.then_inc(sem("xp_full"), 1) if g == NG - 1 and e else tick(ins)
                    dve.wait_ge(sem("xp_hi_ready"), s_ + 1)
                    dve.tensor_tensor(xp_lo[:, :, :].rearrange("p a b -> p (a b)"), xpf.rearrange("p a b -> p (a b)"),
                                      xp_hi[:, :, :].rearrange("p a b -> p (a b)").bitcast(F32), ALU.subtract)\
                       .then_inc(sem("xp_ready"), 1)
                if k == "cmp":
                    dve.wait_ge(sem("cmp_done"), item["s"] + 1)
                    if item["s"] == 0:
                        kcv = bank[4][0:60, 0:DH]
                        tick.step(dve.tensor_copy(kc[0:60, 0, :], kcv))
                        tick.step(dve.tensor_tensor(kc[0:60, 1, :], kc[0:60, 0, :], kc[0:60, 0, :], ALU.mult))
                        dve.tensor_reduce(qss[0:60, 0, 0:1], kc[0:60, 1, :], AX.X, ALU.add).then_inc(sem("qss_ready"), 1)
                        dve.wait_ge(sem("qr_ready"), item["nq"] + 1)
                        tick.step(dve.scalar_tensor_tensor(kc[0:60, 0, :], kc[0:60, 0, :], qr[0:60, 0, 0:1], kg[0:60, 0, :], ALU.mult, ALU.mult))
                        dve.tensor_copy(kc[0:60, 1, :], kc[0:60, 0, :]).then_inc(sem("kc_ready"), 1)
                    else:
                        dve.wait_ge(sem("zeros_ready"), 1)
                        for hh in range(4):
                            rows_ = slice(32 * hh, 32 * hh + 32)
                            ins = dve.tensor_copy(v_bd[rows_, :, DH * hh:DH * hh + DH],
                                                  bank[5][rows_, 0:256].rearrange("p (g d) -> p g d", g=NG))
                            tick(ins) if hh < 3 else ins.then_inc(sem("v_bd_ready"), 1)
                if k == "glu":
                    gi = item["gi"]
                    if item["j"] == 0:
                        dve.memset(v_t[:, :, 0:2], 0.0).then_inc(sem("v_t_ready"), 1)
                    for tt in range(TT):
                        dve.wait_ge(sem("sg_ready"), 2 * gi + tt + 1)
                        dve.scalar_tensor_tensor(glu_a[:, tt, :], bank[tt][:, GC:2 * GC], rstd[:, tt:tt + 1], glu_s[:, tt, :],
                                                 ALU.mult, ALU.mult).then_inc(sem("act_ready"), 1)
                if k == "ffn":
                    f = item["f"]

                    def step(jb, i=None):
                        two = lambda a: 0 if i is None else a * 2 * i

                        def next_lo(q):
                            u = item["unit"] + (2 + 3 * (jb - 1) if jb else 0) + q + RING
                            if u >= len(units) or u < item["have"]:
                                return
                            lo_split(u, unit_raw[u], two)

                        if jb < NJ:
                            next_lo(0)
                            for tt in range(TT):
                                dve.wait_ge(sem("sg_ready"), 2 * (item["gi"] + jb) + tt + 1 + two(2))
                                dve.scalar_tensor_tensor(glu_a[:, tt, :], bank[tt][:, GC:2 * GC], rstd[:, tt:tt + 1] if f else 1.0,
                                                         glu_s[:, tt, :], ALU.mult, ALU.mult).then_inc(sem("act_ready"), 1)
                            for q in ([1, 2] if jb else [1]):
                                next_lo(q)
                            tg = item["tg"] + jb
                            dve.wait_ge(sem("hi_t"), item["hl"] + jb + 1 + two(1))
                            dve.tensor_tensor(f_lo[:, jb % 2, :, :].rearrange("p a b -> p (a b)"), bank[6 + tg % 2][:, :],
                                              f_hi[:, jb % 2, :, :].rearrange("p a b -> p (a b)").bitcast(F32), ALU.subtract)\
                               .then_inc(sem(f"t_free{tg % 2}"), 1)
                        else:
                            u = item["unit"] + 3 * NJ - 1 + RING
                            if u < len(units):
                                lo_split(u, unit_raw[u])
                            for nb in range(2):
                                for tt in range(TT):
                                    if 2 * nb + tt < 3:
                                        dve.wait_ge(sem("d_done"), 3 * f + 2 * nb + tt + 1)
                                    else:
                                        dve.wait_ge(sem("unit_used"), item["unit"] + 3 * NJ)
                                    update(tt, nb, bank[2 + 2 * tt + nb][:, :], "half" if f else 1)

                    first, turns = ffn_loop(item)
                    for j in range(first):
                        step(j)
                    with dve.Fori(0, turns) as i:
                        for h in range(2):
                            step(first + h, i)
                    for j in range(first + 2 * turns, NJ + 1):
                        step(j)

        @block.tensor
        def _(pe):
            def free_pairs(item):
                for q, n in enumerate(item["pairs_before"]):
                    if n:
                        pe.wait_ge(sem(f"pair_free{q}"), n)

            def three(dst, hi, lo, whi, wlo, start, stop):
                pe.matmul(dst, hi, whi, start=start, stop=False)
                pe.matmul(dst, hi, wlo, start=False, stop=False)
                return pe.matmul(dst, lo, whi, start=False, stop=stop)

            def glu_unit(u, half_, need=None, two=lambda a: 0):
                pe.wait_ge(sem("raw_done"), unit_raw[u] + 1 + two(3))
                for kk in range(4):
                    kt = 4 * half_ + kk
                    if need is not None and kt % 2 == 0:
                        wait_group(pe, need[str(kt)])
                    wv = [r_[:, u % RING, 512 * kk:512 * kk + 512] for r_ in (w_hi, w_lo)]
                    for tt in range(TT):
                        ins = three(bank[tt][:, :], h_hi[:, kt, tt * P:(tt + 1) * P], h_lo[:, kt, tt * P:(tt + 1) * P],
                                    wv[0], wv[1], kt == 0, kt == KT - 1)
                return ins

            def glu_transposes(tg, gi, two=lambda a: 0, one=0):
                if tg >= 2:
                    pe.wait_ge(sem(f"t_free{tg % 2}"), tg // 2 + one)
                for tt in range(TT):
                    pe.wait_ge(sem("act_ready"), 2 * gi + tt + 1 + two(2))
                    for kk in range(2):
                        ins = pe.transpose(bank[6 + tg % 2][:, kk * T + tt * P:kk * T + (tt + 1) * P],
                                           glu_a[:, tt, kk * P:(kk + 1) * P], ident)
                ins.then_inc(sem("t_done"), 1)

            for item in plan:
                k = item["kind"]
                if k == "init":
                    pe.wait_ge(sem("const_full"), 16)
                    pe.wait_ge(sem("rows_full"), 16 * 9)
                    pe.transpose(bank[6][:, 0:P], rows1[:, :], ident)
                    pe.transpose(bank[7][:, 0:56], rows2[0:56, :], ident[0:56, 0:56])
                    pe.transpose(bank[5][:, 0:KT], rows2[0:KT, :], ident[0:KT, 0:KT]).then_inc(sem("init_done"), 1)
                    pe.wait_ge(sem("c_ready"), 1)
                    pe.wait_ge(sem("cols_ready"), 1)
                if k == "lin":
                    st, c, part, u, pi = item["stage"], item["chunk"], item["part"], item["unit"], item["pi"]
                    pe.wait_ge(sem("raw_done"), unit_raw[u] + 1)
                    b = [bank[2 * (pi % 2) + tt] for tt in range(TT)]
                    if part == 0:
                        if item["pair_before"]:
                            pe.wait_ge(sem(f"pair_free{pi % 2}"), item["pair_before"])
                    if st == "cm":
                        pe.wait_ge(sem("xp_ready"), c + 1)
                        if part == 0:
                            pe.wait_ge(sem("small_full"), 16 * 4)
                            pe.matmul(b[0][0:60, 0:256], ones[0:1, 0:60], b1r[0:1, c, :], start=True, stop=False)
                        for kk in range(8):
                            kt = 8 * part + kk
                            wv = [r_[:, u % RING, 256 * kk:256 * kk + 256] for r_ in (w_hi, w_lo)]
                            ins = three(b[0][0:60, 0:256], xp_hi[:, kt, :], xp_lo[:, kt, :], wv[0], wv[1], False, kt == 15)
                        ins.then_inc(sem("unit_used"), 1)
                        continue
                    n = {"ki": 72, "gn": 48}.get(st, 512)
                    k0 = {"ba": 0, "bb": 4}.get(st, 4 * part)
                    kts = range(KT) if n < 512 else range(k0, k0 + 4)
                    single = st in ("ki", "gn", "ba", "bb")
                    for q, kt in enumerate(kts):
                        if kt % 2 == 0:
                            wait_group(pe, item["need"][str(kt)])
                        wv = [r_[:, u % RING, n * q:n * q + n] for r_ in (w_hi, w_lo)]
                        for tt in range(TT):
                            first_ = q == 0 and (single or part == 0)
                            last_ = q == len(kts) - 1 and (single or part == 1)
                            ins = three(b[tt][:, 0:n], h_hi[:, kt, tt * P:(tt + 1) * P], h_lo[:, kt, tt * P:(tt + 1) * P],
                                        wv[0], wv[1], first_, last_)
                    ins.then_inc(sem("unit_used"), 1)
                if k == "tp":
                    st, tg, g = item["stage"], item["tg"], item["g"]
                    b = bank[6 + tg % 2]
                    wait_bank(pe, tg)
                    if st == "mod":
                        pe.wait_ge(sem("raw_done"), find["raw", g] + 1)
                        a = acc[:, g % 2, :]
                        if g // 2 in (2, 5):
                            i5 = g // 2 // 3
                            pe.wait_ge(sem("b_row_full"), 16 * (i5 + 1))
                            pe.matmul(b[:, :], ones, a, start=True, stop=False)
                            ins = pe.matmul(b[:, :], ones[0:1, :], b_row[0:1, 512 * (g % 2):512 * (g % 2) + 512],
                                            start=False, stop=True)
                        else:
                            for q in range(4):
                                ins = pe.matmul(b[:, q:q + 1], a[:, q * P:(q + 1) * P], ones[:, 0:1], start=True, stop=True)
                    elif st in ("norm", "normf", "o", "merged", "on"):
                        if st == "norm":
                            pe.wait_ge(sem("x_ready"), 4 * xu[item["norm"]] - (2 if g < 2 else 0))
                            src = x
                        elif st == "normf":
                            pe.wait_ge(sem("xn_ready"), 2 * (item["norm"] + 1))
                            src = o1
                        elif st == "o":
                            pe.wait_ge(sem("o_ready"), 16)
                            src = o1
                        elif st == "on":
                            pe.wait_ge(sem("o_ready"), 80)
                            src = o2
                        else:
                            for c_ in range(2):
                                wait_pair(pe, find["pi", "bb", c_])
                            src = sig[:, :, 0, :]
                        for kk in range(2):
                            for tt in range(TT):
                                at = (2 * g + kk) * P
                                ins = pe.transpose(b[:, kk * T + tt * P:kk * T + (tt + 1) * P], src[:, tt, at:at + P], ident)
                    elif st in ("qb", "kb", "qa", "ka", "qi"):
                        pe.wait_ge(sem("rope_done"), ("qi", "qb", "kb", "qa", "ka").index(st) + 1)
                        for kk in range(2):
                            for tt in range(TT):
                                at = (2 * g + kk) * P
                                ins = pe.transpose(b[:, kk * T + tt * P:kk * T + (tt + 1) * P], ro[:, tt, at:at + P], ident)
                    elif st == "ki":
                        pe.wait_ge(sem("kid_ready"), 1)
                        for tt in range(TT):
                            ins = pe.transpose(b[:, tt * P:(tt + 1) * P], kid[:, tt, :], ident)
                    elif st == "cb":
                        wait_pair(pe, find["pi", "cb", g // 2])
                        for kk in range(2):
                            for tt in range(TT):
                                at = (2 * g + kk) * P
                                ins = pe.transpose(b[:, kk * T + tt * P:kk * T + (tt + 1) * P], b_s[:, tt, at:at + P], ident)
                    elif st == "kvt":
                        if item["c"] == 0:
                            wait_pair(pe, find["pi", "kv", 0])
                            s_, g0 = divmod(2 * g, NG)
                            srcs = [kv_d[:, tt, s_, g0 + kk, :, :] for kk in range(2) for tt in range(TT)]
                        else:
                            pe.wait_ge(sem("kd_done"), item["c"])
                            srcs = [kd[:, tt, 2 * g + kk, :, :] for kk in range(2) for tt in range(TT)]
                        for q, s_ in enumerate(srcs):
                            ins = pe.transpose(b[:, q * P:(q + 1) * P], s_.rearrange("p a b -> p (a b)"), ident)
                    elif st == "qn":
                        wait_pair(pe, find["pi", "qg", item["c"]])
                        for kk in range(2):
                            for tt in range(TT):
                                at = (2 * g + kk) * P
                                ins = pe.transpose(b[:, kk * T + tt * P:kk * T + (tt + 1) * P], pqn[:, tt, at:at + P], ident)
                    elif st == "hc":
                        wait_pair(pe, find["pi", "cm", item["c"]])
                        for kk in range(2):
                            ins = pe.transpose(b[:, kk * 60:(kk + 1) * 60], hc[0:60, kk * P:(kk + 1) * P], ident[0:60, 0:60])
                    elif st == "kc":
                        pe.wait_ge(sem("kc_ready"), 1)
                        ins = pe.transpose(b[:, 0:60], kc[0:60].rearrange("p a b -> p (a b)"), ident[0:60, 0:60])
                    elif st == "pc":
                        pe.wait_ge(sem("pc_ready"), item["tt"] + 1)
                        for g_ in range(NG):
                            ins = pe.transpose(b[:, g_ * P:(g_ + 1) * P], pc[:, 4 * g_:4 * g_ + 4, :].rearrange("p a b -> p (a b)"), ident)
                    elif st == "p":
                        pe.wait_ge(sem("exp_done"), item["it"] + 1)
                        if item["it"] >= 2:
                            pe.wait_ge(sem("o_ready"), item["it"] - 1)
                        for kk in range(item["tt"] + 1):
                            ins = pe.transpose(b[:, kk * P:(kk + 1) * P], p_s[:, item["it"] % 2, kk * P:(kk + 1) * P], ident)
                    ins.then_inc(sem("t_done"), 1)
                if k == "ix":
                    n, tt, pr = P * (item["tt"] + 1), item["tt"], item["pair"]
                    if item["n"] == 0:
                        pe.wait_ge(sem("o_ready"), 8)
                    else:
                        pe.wait_ge(sem("rl_ready"), 2 * item["n"])
                    for hh in range(2):
                        r_ = slice(64 * hh, 64 * hh + 64)
                        ins = pe.matmul(bank[4 + hh][:, 0:n], qi_t[r_, pr, tt * P:(tt + 1) * P], ki_t[r_, 0:n], start=True, stop=True)
                    ins.then_inc(sem("ix_done"), 1)
                if k == "qk":
                    it, tt, h = item["it"], item["tt"], item["h"]
                    n = P * (tt + 1)
                    if it == 8:
                        pe.wait_ge(sem("rl_ready"), 16)
                    if it == 16:
                        pe.wait_ge(sem("oc_ready"), 2)
                    if it >= 2:
                        pe.wait_ge(sem("sm_done"), it - 1)
                    if it in (0, 8):
                        for st in ("qb", "kb") if it == 0 else ("qa", "ka"):
                            for g in range(2):
                                wait_group(pe, find["tg", st, g])
                    if item["b"] in ("dsa", "moba"):
                        lhs, rhs = q_t[:, h, tt * P:(tt + 1) * P], k_t[:, h, 0:n]
                    else:
                        r_ = slice(64 * (h % 2), 64 * (h % 2) + 64)
                        br = 0 if item["b"] == "sel" else 1
                        lhs, rhs = q_n[r_, h // 2, tt * P:(tt + 1) * P], kn_t[r_, br, h // 4, 0:n]
                    pe.matmul(bank[4 + it % 2][:, 0:n], lhs, rhs, start=True, stop=True).then_inc(sem("qk_done"), 1)
                if k == "pv":
                    it, tt, h = item["it"], item["tt"], item["h"]
                    wait_group(pe, find["tg", "p", it])
                    if item["b"] in ("dsa", "moba"):
                        if it in (0, 8):
                            wait_pair(pe, find["pi", "vb" if it == 0 else "va", 0])
                        wv = lambda kk: v_s[:, kk, HD * h:HD * h + HD]
                        w_ = HD
                    else:
                        br = 0 if item["b"] == "sel" else 1
                        wv = lambda kk: vn_s[:, br, kk, DH * (h // 4):DH * (h // 4) + DH]
                        w_ = DH
                    for kk in range(tt + 1):
                        ins = pe.matmul(bank[6 + find["tg", "p", it] % 2][:, T:T + w_], pt_s[:, it % 2, kk * P:(kk + 1) * P], wv(kk),
                                        start=kk == 0, stop=kk == tt)
                    ins.then_inc(sem("pv_done"), 1)
                if k == "cmp":
                    wait_group(pe, find["tg", "hc", (item["s"], 0)])
                    if item["s"] == 0:
                        for kk in range(2):
                            ins = pe.matmul(bank[4][0:60, 0:DH], hc_t[:, kk, :], w2[:, 0, kk, :], start=kk == 0, stop=kk == 1)
                    else:
                        for g in range(NG):
                            for kk in range(2):
                                ins = pe.matmul(bank[5][:, DH * g:DH * g + DH], hc_p[:, kk, g, :, :].rearrange("p a b -> p (a b)"),
                                                w2[:, 1, kk, :], start=kk == 0, stop=kk == 1)
                    ins.then_inc(sem("cmp_done"), 1)
                if k == "cs":
                    tt = item["tt"]
                    if tt == 0:
                        wait_group(pe, find["tg", "kc", 0])
                        for g in range(2):
                            wait_group(pe, find["tg", "qn", (1, g)])
                        pe.wait_ge(sem("v_bd_ready"), 1)
                        pe.wait_ge(sem("kc_ready"), 1)
                    else:
                        pe.wait_ge(sem("oc_ready"), tt)
                    for h in range(NQ):
                        r_ = slice(64 * (h % 2), 64 * (h % 2) + 64)
                        g = h // 4
                        ins = pe.matmul(bank[4 + h % 2][:, 16 * (h // 2):16 * (h // 2) + NC], q_n[r_, h // 2, tt * P:(tt + 1) * P],
                                        kc_t[r_, NC * g:NC * g + NC], start=True, stop=True)
                    ins.then_inc(sem("cs_done"), 1)
                if k == "co_":
                    tt = item["tt"]
                    wait_group(pe, find["tg", "pc", (tt, 0)])
                    for g in range(NG):
                        ins = pe.matmul(bank[4 + g // 2][:, 256 * (g % 2):256 * (g % 2) + 256], pc_t[:, g, :], v_bd[:, g, :],
                                        start=True, stop=True)
                    ins.then_inc(sem("cv_done"), 1)
                if k == "glu":
                    u, gi = item["unit"], item["gi"]
                    if item["j"] == 0:
                        free_pairs(item)
                    glu_unit(u, 0, item["need"] if item["j"] == 0 else None).then_inc(sem("unit_used"), 1)
                    glu_unit(u + 1, 1, item["need"] if item["j"] == 0 else None).then_inc(sem("unit_used"), 1)
                    glu_transposes(item["tg"], gi)
                if k == "ffn":
                    f = item["f"]

                    def step(jb, i=None):
                        two = lambda a: 0 if i is None else a * 2 * i
                        u = item["unit"] + (2 + 3 * (jb - 1) if jb else 0)
                        if jb < NJ:
                            need = item["need"] if jb == 0 else None
                            glu_unit(u, 0, need, two).then_inc(sem("unit_used"), 1)
                            glu_unit(u + 1, 1, need, two).then_inc(sem("unit_used"), 1)
                            u += 2
                        if jb > 0:
                            tg = item["tg"] + jb - 1
                            pe.wait_ge(sem("raw_done"), unit_raw[u] + 1 + two(3))
                            pe.wait_ge(sem(f"t_free{tg % 2}"), tg // 2 + 1 + (0 if i is None else i))
                            fb = (jb - 1) % 2
                            order = [(nb, tt) for nb in range(2) for tt in range(TT)] if jb == NJ else \
                                    [(nb, tt) for tt in range(TT) for nb in range(2)]
                            if jb == NJ:
                                for n_, (nb, tt) in enumerate(order):
                                    for kk in range(2):
                                        ins = three(bank[2 + 2 * tt + nb][:, :], f_hi[:, fb, kk, tt * P:(tt + 1) * P], f_lo[:, fb, kk, tt * P:(tt + 1) * P],
                                                    w_hi[:, u % RING, D * kk + 512 * nb:D * kk + 512 * nb + 512],
                                                    w_lo[:, u % RING, D * kk + 512 * nb:D * kk + 512 * nb + 512], False, kk == 1)
                                    ins.then_inc(sem("d_done" if n_ < 3 else "unit_used"), 1)
                            else:
                                for kk in range(2):
                                    for nb, tt in order:
                                        ins = three(bank[2 + 2 * tt + nb][:, :], f_hi[:, fb, kk, tt * P:(tt + 1) * P], f_lo[:, fb, kk, tt * P:(tt + 1) * P],
                                                    w_hi[:, u % RING, D * kk + 512 * nb:D * kk + 512 * nb + 512],
                                                    w_lo[:, u % RING, D * kk + 512 * nb:D * kk + 512 * nb + 512], jb == 1 and kk == 0, False)
                                ins.then_inc(sem("unit_used"), 1)
                        if jb < NJ:
                            glu_transposes(item["tg"] + jb, item["gi"] + jb, two, 0 if i is None else i)

                    free_pairs(item)
                    first, turns = ffn_loop(item)
                    for j in range(first):
                        step(j)
                    with pe.Fori(0, turns) as i:
                        for h in range(2):
                            step(first + h, i)
                    for j in range(first + 2 * turns, NJ + 1):
                        step(j)


_INS = ["x", "c", "w_mod", "b_mod", "g_mix_norm", "g_ffn_norm", "w_in", "g_q_dsa", "g_k_dsa", "g_q_moba", "g_k_moba",
        "w_br_dsa", "w_br_moba", "w_out", "w_gate_up", "w_down", "ffn_norm_2", "ffn_w_gate_up_2", "ffn_w_down_2",
        "mix_norm_2", "conv_w_in_2", "conv_w_2", "conv_w_out_2", "kv_norm_2", "kv_w_2", "cmp_pos_2", "cmp_w1_2",
        "cmp_b1_2", "cmp_w2_2", "k_norm_2", "nsa_w_qg_2", "q_norm_2", "nsa_w_o_2"]


def kernel(**inputs):
    import numpy as _np
    import concourse.bacc as _bacc
    from concourse import mybir as _mybir
    from concourse.bass_utils import run_bass_kernel_spmd as _run

    nc = _bacc.Bacc("TRN2", target_bir_lowering=False, num_devices=1)
    arrays, args = {}, {}
    for name in _INS:
        a = _np.ascontiguousarray(inputs[name])
        arrays[f"in_{name}_dram"] = a
        args[name] = nc.dram_tensor(f"in_{name}_dram", a.shape, _mybir.dt.from_np(a.dtype), kind="ExternalInput").ap()
    arrays["const_dram"] = constant_table()
    args["const"] = nc.dram_tensor("const_dram", (P, C_END), F32, kind="ExternalInput").ap()
    out = nc.dram_tensor("out_0_dram", (T, D), F32, kind="ExternalOutput").ap()
    two_block_program(nc, args, out)
    r = _run(nc, [arrays], core_ids=[0])
    return r.results[0]["out_0_dram"].reshape(1, T, D)
```

```python
from contextlib import ExitStack

import numpy as np

import concourse.bass as bass
from concourse import mybir

ALU = mybir.AluOpType
ACT = mybir.ActivationFunctionType
F32 = mybir.dt.float32
F32R = mybir.dt.float32r
AX = mybir.AxisListType

P = 128
T = 256
TT = T // P
D = 1024
KT = D // P
FF = 2816
GC = 256
NJ = FF // GC
UNIT = 2048
RING = 3
EARLY = 6
HD = 128
NH = 4
IH, ID = 8, 64
TOPK = 64
NQ, DH, NG = 16, 64, 4
CB, CS = 32, 16
NC = (T - CB) // CS + 1
EPS = 1e-6
NEG = -1e30
TAKEN = -3e38
HI_SCALE = (IH ** -0.5) * (ID ** -0.5)

C_ID, C_ONE, C_COSH, C_SINH = 0, 128, 256, 512
C_COSI, C_SINI, C_MASK, C_CM, C_CV, C_END = 768, 896, 1024, 1280, 1312, 1344


def constant_table():
    t = np.zeros((P, C_END), np.float32)
    t[:, C_ID:C_ID + P] = np.eye(P, dtype=np.float32)
    t[:, C_ONE:C_ONE + P] = 1.0
    for dim, at_cos, at_sin in ((HD, C_COSH, C_SINH), (ID, C_COSI, C_SINI)):
        inv = np.float32(10000.0) ** (-np.arange(0, dim, 2, dtype=np.float32) / np.float32(dim))
        ang = np.arange(T, dtype=np.float32)[:, None] * inv[None, :].astype(np.float32)
        cos, sin = np.cos(ang).astype(np.float32), np.sin(ang).astype(np.float32)
        for tt in range(TT):
            rows = slice(tt * P, (tt + 1) * P)
            t[:, at_cos + tt * dim:at_cos + (tt + 1) * dim] = np.concatenate([cos[rows], cos[rows]], 1)
            t[:, at_sin + tt * dim:at_sin + (tt + 1) * dim] = np.concatenate([-sin[rows], sin[rows]], 1)
    q, k = np.arange(P)[:, None], np.arange(P)[None, :]
    t[:, C_MASK + P:C_MASK + 2 * P] = np.where(k <= q, 0.0, NEG)
    end = np.arange(NC) * CS + CB - 1
    for tt in range(TT):
        ok = end[None, :] <= (np.arange(P) + tt * P)[:, None]
        t[:, C_CM + tt * 16:C_CM + tt * 16 + NC] = np.where(ok, 0.0, -NEG)
        t[:, C_CV + tt * 16:C_CV + tt * 16 + NC] = ok
    return t


def make_plan():
    plan, units = [], []

    def add(kind, **a):
        item = dict(a, kind=kind)
        plan.append(item)
        return item

    def lin(stage, chunk, parts, before_evac=()):
        for part in range(parts):
            add("lin", stage=stage, chunk=chunk, part=part, parts=parts, unit=len(units))
            units.append((stage, chunk, part))
        plan.extend(before_evac)
        add("evac", stage=stage, chunk=chunk)

    def tgroup(stage, n, **a):
        return [dict(a, kind="tp", stage=stage, g=g) for g in range(n)]

    def ffn(f, stage, norm):
        add("ffn", f=f, stage=stage, norm=norm, unit=len(units))
        for j in range(NJ + 1):
            if j < NJ:
                units.extend([(stage, j, 0), (stage, j, 1)])
            if j > 0:
                units.append((stage + "_d", j - 1, 0))

    def norm(n, plain):
        if plain:
            plan.extend(tgroup("norm", 4, norm=n))
            add("square")
        else:
            add("square")
            add("scale_x", norm=n)
            plan.extend(tgroup("normf", 4, norm=n))

    def attention(items):
        steps = []
        for i in range(len(items) + 2):
            s = []
            if i < len(items):
                s += [dict(items[i], kind="qk"), dict(items[i], kind="sm")]
            if 1 <= i <= len(items):
                s.append(dict(items[i - 1], kind="tp", stage="p", g=0))
            if i >= 2:
                s.append(dict(items[i - 2], kind="pv"))
            steps.append(s)
        return steps

    def part(stage, chunk, number, parts, after=(), inside=()):
        subs = len(inside) if inside else 1
        for q in range(subs):
            add("lin", stage=stage, chunk=chunk, part=number, parts=parts, unit=len(units), sub=q, subs=subs)
            if inside:
                plan.extend(inside[q])
        units.append((stage, chunk, number))
        for a in after:
            plan.extend(a)
        add("then split", unit=len(units) - 1)

    def evac(stage, chunk=0):
        return [dict(kind="evac", stage=stage, chunk=chunk)]

    def mod(m, half):
        return [dict(kind="mod", m=m, half=half)]

    def mod_sum(m):
        return [dict(kind="tp", stage="mod", g=m)]

    def topk(tt, piece):
        return [dict(kind="topk", tt=tt, piece=piece)]

    def spread(steps, parts):
        n = 4 * parts
        quarters = [sum(steps[k * len(steps) // n:(k + 1) * len(steps) // n], []) for k in range(n)]
        return [quarters[4 * p_:4 * p_ + 4] for p_ in range(parts)]

    index = [[[dict(kind="ix", tt=tt, pair=pr)] for pr in range(4)] for tt in range(TT)]
    add("init")
    plan.extend(mod(1, 0) + mod(1, 1) + mod(0, 0) + mod(0, 1) + mod_sum(1))
    add("square")
    plan.extend(mod(2, 0) + mod(2, 1))
    add("scale_x", norm=0)
    plan.extend(mod(3, 0) + mod(3, 1) + mod_sum(0) + mod_sum(2) + mod_sum(3))
    add("mod_a", norm=0)
    add("then split", unit=-RING)
    plan.extend(tgroup("normf", 2, norm=0))
    add("then split", unit=1 - RING)
    plan.extend(tgroup("normf", 4, norm=0)[2:])
    part("ki", 0, 0, 1)
    part("qi", 0, 0, 2, [evac("ki"), mod(4, 0)])
    part("qi", 0, 1, 2, [tgroup("ki", 1), mod(4, 1)])
    part("qb", 0, 0, 2, [evac("qi"), mod_sum(4), mod(5, 0)])
    part("qb", 0, 1, 2, [tgroup("qi", 2), mod(5, 1)])
    part("kb", 0, 0, 2, [evac("qb"), mod_sum(5)])
    part("kb", 0, 1, 2, [tgroup("qb", 2), mod(6, 0)], index[0])
    part("vb", 0, 0, 2, [evac("kb"), mod(6, 1)])
    part("vb", 0, 1, 2, [tgroup("kb", 2), mod(7, 0)], index[1])
    steps = attention([dict(b="moba", h=h, tt=tt) for h in range(NH) for tt in range(TT)])
    inside = spread(steps, 4)
    part("ga", 0, 0, 2, [mod(7, 1)], [evac("vb") + inside[0][0], *inside[0][1:]])
    part("ga", 0, 1, 2, [topk(0, 0)], inside[1])
    part("ga", 1, 0, 2, [evac("ga"), topk(0, 1)], inside[2])
    part("ga", 1, 1, 2, [mod_sum(6), mod(8, 0)], inside[3])
    part("qa", 0, 0, 2, [evac("ga", 1), mod_sum(7), topk(0, 2), topk(0, 3), mod(8, 1)])
    part("qa", 0, 1, 2, [mod(9, 0), topk(1, 0)])
    part("ka", 0, 0, 2, [evac("qa"), mod_sum(8)])
    part("ka", 0, 1, 2, [tgroup("qa", 2), topk(1, 1), mod(9, 1)])
    part("va", 0, 0, 2, [evac("ka"), mod_sum(9)])
    part("va", 0, 1, 2, [tgroup("ka", 2), topk(1, 2), topk(1, 3), mod(10, 0)])
    steps = attention([dict(b="dsa", h=h, tt=tt) for h in range(NH) for tt in range(TT)])
    inside = spread(steps, 4)
    part("gb", 0, 0, 2, [mod(10, 1)], [evac("va") + inside[0][0], *inside[0][1:]])
    part("gb", 0, 1, 2, [mod(11, 0)], inside[1])
    part("gb", 1, 0, 2, [evac("gb"), mod(11, 1)], inside[2])
    part("gb", 1, 1, 2, [], inside[3])
    plan.extend(evac("gb", 1))
    add("sigmoid")
    plan.extend(tgroup("o", 4))
    part("ba", 0, 0, 1, [mod_sum(10)])
    part("ba", 1, 0, 1, [evac("ba", 0), mod_sum(11)])
    part("bb", 0, 0, 1, [evac("ba", 1)])
    part("bb", 1, 0, 1, [evac("bb", 0)])
    plan.extend(evac("bb", 1))
    add("mod_a", norm=1)
    plan.extend(tgroup("merged", 4))
    for c in range(2):
        lin("out1", c, 2)
    norm(1, False)
    ffn(0, "f0", 1)
    norm(2, True)
    ffn(1, "f1", 2)
    norm(3, True)
    for j in range(4):
        add("glu", j=j, unit=len(units))
        units.extend([("cv", j, 0), ("cv", j, 1)])
    conv = [[dict(kind="conv", g=g)] for g in range(4)]
    part("cb", 0, 0, 2, [conv[0]])
    part("cb", 0, 1, 2, [conv[1]])
    part("cb", 1, 0, 2, [evac("cb", 0), conv[2]])
    part("cb", 1, 1, 2, [conv[3]])
    plan.extend(evac("cb", 1))
    plan.extend(tgroup("cb", 4))
    for c in range(2):
        lin("co", c, 2)
    norm(4, True)
    ffn(2, "f2", 4)
    norm(5, True)
    for c in range(3):
        lin("kv", c, 2, before_evac=[dict(kind="tp", stage="kvt", g=g, c=c - 1) for g in range([0, 4, 2][c])])
    norm(6, True)
    plan.extend([dict(kind="tp", stage="kvt", g=g, c=2) for g in range(2)])
    ffn(3, "f3", 6)
    add("xp", s=0)
    part("cm", 0, 0, 2)
    part("cm", 0, 1, 2)
    plan.extend(evac("cm", 0))
    add("xp", s=1)
    part("cm", 1, 0, 2, [[dict(kind="tp", stage="hc", g=0, c=0), dict(kind="cmp", s=0)]])
    part("cm", 1, 1, 2)
    plan.extend(evac("cm", 1))
    plan.append(dict(kind="tp", stage="hc", g=0, c=1))
    add("cmp", s=1)
    plan.append(dict(kind="tp", stage="kc", g=0))
    norm(7, True)
    lin("qg", 0, 2)
    lin("gn", 0, 1)
    lin("qg", 1, 2, before_evac=tgroup("qn", 2, c=0))
    plan.extend(tgroup("qn", 2, c=1))
    for tt in range(TT):
        add("cs", tt=tt)
        plan.append(dict(kind="tp", stage="pc", g=0, c=tt, tt=tt))
        add("co_", tt=tt)
    att = [dict(b=b, h=h, tt=tt) for h in range(NQ) for tt in range(TT) for b in ("sel", "win")]
    for step in attention(att):
        plan.extend(step)
    plan.extend(tgroup("on", 4))
    for c in range(2):
        lin("wo", c, 2)
    norm(8, True)
    ffn(4, "f4", 8)
    full, s = [], 0

    def split(upto):
        nonlocal s
        while s <= upto and s < len(units):
            full.append(dict(kind="split", unit=s))
            s += 1

    for item in plan:
        if item["kind"] == "lin" and item["unit"] == 0:
            split(RING - 1)
        if item["kind"] == "then split":
            split(item["unit"] + RING)
            continue
        full.append(item)
        if item["kind"] == "lin" and "sub" not in item:
            split(item["unit"] + RING)
        if item["kind"] == "glu":
            split(item["unit"] + 1 + RING)
        if item["kind"] == "ffn":
            n = 3 * NJ
            item["have"] = s
            s = min(item["unit"] + n + RING, len(units))
    count = {}

    def number(key, n=1):
        count[key] = count.get(key, 0) + n
        return count[key] - n

    raw = []
    unit_raw, pair_after, pi_of = {}, {}, {}
    last_p = None
    for item in full:
        k = item["kind"]
        item["n"] = number("kind " + k)
        if k == "split":
            unit_raw[item["unit"]] = len(raw)
            raw.append(("unit", item["unit"]))
        if k == "mod":
            item["raw"] = len(raw)
            item["by"] = "pool" if item["m"] >= 4 else "dve" if item["m"] else "pe"
            item["of"] = number("mod by " + item["by"])
            raw.append(("mod", item["m"], item["half"], item["by"], item["of"]))
        if k == "lin" and item["part"] == 0 and item.get("sub", 0) == 0:
            pi_of[item["stage"], item["chunk"]] = item["pi"] = number("pi")
            item["pair_before"] = count.get(f"pair{item['pi'] % 2}", 0)
        elif k in ("lin", "evac"):
            item["pi"] = pi_of[item["stage"], item["chunk"]]
        if k == "evac":
            st = item["stage"]
            if st not in ("out1", "co", "wo"):
                pair_after[item["pi"]] = number(f"pair{item['pi'] % 2}") + 1
            if st in ("qi", "qb", "kb", "qa", "ka"):
                item["rope"] = number("rope")
            if st in ("qb", "kb", "qa", "ka", "qg") or (st == "kv" and item["chunk"]):
                item["nq"] = number("nq")
        if k == "cmp" and item["s"] == 0:
            item["nq"] = number("nq")
        if k == "tp":
            item["tg"] = number("tg")
            if item["stage"] in PAIRED:
                item["hl"] = number("hl")
            if item["stage"] != "p" and last_p is not None and item["tg"] - last_p[0] <= 2:
                item["outputs"] = last_p[1] + 1
            if item["stage"] == "p":
                last_p = item["tg"], count.get("it tp", 0)
        if k == "ffn":
            item["tg"], item["hl"], item["gi"] = number("tg", NJ), number("hl", NJ), number("gi", NJ)
            for u in range(item["have"], min(item["unit"] + 3 * NJ + RING, len(units))):
                unit_raw[u] = len(raw)
                raw.append(("unit", u))
        if k == "glu":
            item["tg"], item["gi"] = number("tg"), number("gi")
        if k in ("ffn", "glu"):
            item["pairs_before"] = [count.get(f"pair{q}", 0) for q in range(2)]
        if k in ("qk", "sm", "pv") or (k == "tp" and item["stage"] == "p"):
            item["it"] = number("it " + k)
    find, made = {}, {}
    for item in full:
        k, st = item["kind"], item.get("stage")
        if k == "tp":
            key = item["it"] if st == "p" else (item["c"], item["g"]) if "c" in item else item["g"]
            find["tg", st, key] = item["tg"]
            if st in ("norm", "normf", "o", "merged", "on", "cb"):
                made = dict(made, **{str(2 * item["g"] + q): item["tg"] for q in range(2)})
        if k == "lin":
            find["pi", st, item["chunk"]] = item["pi"]
            find["unit", st, item["chunk"]] = item["unit"]
        if k == "glu":
            find["glu tg"] = item["tg"]
        if k == "mod":
            find["mod", item["m"]] = item["by"], item["of"]
            find["raw", item["m"]] = item["raw"]
        if k in ("lin", "ffn", "glu"):
            item["need"] = made
    freed = [("raw_done", r[1] + 1) if r[0] == "unit" else ("mod_used_" + r[3], r[4] + 1) for r in raw]
    return full, units, raw, unit_raw, find, pair_after, freed


def turn(r):
    return (r - EARLY) // RING + 1


PAIRED = ("norm", "normf", "o", "merged", "on")


def two_block_program(nc, A, out):
    plan, units, raws, unit_raw, find, pair_after, freed = make_plan()

    def rows(w):
        return w.rearrange("(k p) n -> p k n", p=P)

    w_mod, w_in = rows(A["w_mod"][0]), rows(A["w_in"][0])
    gate_up = [rows(A["w_gate_up"][0])] + [rows(A["ffn_w_gate_up_2"][l, i]) for l in range(2) for i in range(2)]
    down = [rows(A["w_down"][0])] + [rows(A["ffn_w_down_2"][l, i]) for l in range(2) for i in range(2)]
    in_at = dict(qa=0, ka=512, va=1024, qi=1536, ki=2048, qb=2120, kb=2632, vb=3144, ga=3656, gb=4680)
    plain = dict(ba=A["w_br_dsa"][0], bb=A["w_br_moba"][0], out1=A["w_out"][0], co=A["conv_w_out_2"][0],
                 kv=A["kv_w_2"], wo=A["nsa_w_o_2"][0])

    def unit_source(u):
        stage, c, part = units[u]
        ks = slice(4 * part, 4 * part + 4)
        if stage in in_at:
            if stage == "ki":
                return w_in[:, :, in_at["ki"]:in_at["ki"] + ID + IH], KT * (ID + IH)
            at = in_at[stage] + 512 * c
            return w_in[:, ks, at:at + 512], UNIT
        if stage in plain:
            return rows(plain[stage])[:, ks, 512 * c:512 * c + 512], UNIT
        if stage == "cb":
            return rows(A["conv_w_in_2"][0])[:, ks, 512 * c:512 * c + 512], UNIT
        if stage == "cv":
            v = rows(A["conv_w_in_2"][0])[:, ks, D:3 * D].rearrange("p k (s n) -> p k s n", s=2)
            return v[:, :, :, GC * c:GC * c + GC], UNIT
        if stage == "qg":
            return rows(A["nsa_w_qg_2"][0])[:, ks, 512 * c:512 * c + 512], UNIT
        if stage == "gn":
            return rows(A["nsa_w_qg_2"][0])[:, :, D:D + 48], KT * 48
        if stage == "cm":
            return rows(A["cmp_w1_2"][c])[:, 8 * part:8 * part + 8, :], UNIT
        f = int(stage[1])
        if stage.endswith("_d"):
            return down[f][:, 2 * c:2 * c + 2, :], UNIT
        return gate_up[f][:, ks, :].rearrange("p k (s n) -> p k s n", s=2)[:, :, :, GC * c:GC * c + GC], UNIT

    with ExitStack() as ctx:
        def sb(name, shape, dt=F32):
            return ctx.enter_context(nc.sbuf_tensor(name, [P, *shape], dt))

        sems = {}

        def sem(name):
            if name not in sems:
                sems[name] = ctx.enter_context(nc.semaphore(name))
            return sems[name]

        raw = sb("raw_ring", [RING, UNIT])
        w_hi = sb("w_hi_ring", [RING, UNIT], F32R)
        w_lo = sb("w_lo_ring", [RING, UNIT], F32R)
        h_hi = sb("h_hi", [KT, T], F32R)
        h_lo = sb("h_lo", [KT, T], F32R)
        f_hi = sb("f_hi", [2, 2, T], F32R)
        f_lo = sb("f_lo", [2, 2, T], F32R)
        xp_hi = sb("xp_hi", [16, 60], F32R)
        xp_lo = sb("xp_lo", [16, 60], F32R)
        x = sb("x", [TT, D])
        const = sb("const", [C_END])
        glu_s = sb("glu_s", [TT, GC])
        glu_a = sb("glu_a", [TT, GC])
        junk = sb("junk", [D])
        rows1 = sb("rows1", [P])
        rows2 = sb("rows2", [P])
        cols1 = sb("cols1", [P])
        cols2 = sb("cols2", [56])
        c_act = sb("c_act", [KT])
        modc = sb("modc", [2, 16])
        mod_s = sb("mod_s", [2, KT])
        ss = sb("ss", [TT])
        rstd = sb("rstd", [TT])
        qss = sb("qss", [TT, 8])
        qr = sb("qr", [TT, 8])
        half = sb("half", [16])
        rq = sb("rq", [2, TT, NH])
        rqn = sb("rqn", [TT, NQ])
        mn = sb("mn", [80])
        sm = sb("sm", [80])
        rc = sb("rc", [80])
        top8 = sb("top8", [8])
        arena_size = (nc.sbuf_bytes_remaining() if callable(nc.sbuf_bytes_remaining) else nc.sbuf_bytes_remaining) // 4 - 64
        arena = sb("arena", [arena_size])
        used = [0]

        def carve(*shape):
            n = int(np.prod(shape))
            v = arena[:, used[0]:used[0] + n]
            used[0] += n
            assert used[0] <= arena_size, (used[0], arena_size)
            if len(shape) == 1:
                return v
            names = "abcd"[:len(shape)]
            return v.rearrange(f"p ({' '.join(names)}) -> p {' '.join(names)}",
                               **{k: s for k, s in zip(names[1:], shape[1:])})

        s_s = carve(2, T)
        p_s = carve(2, T)
        pt_s = carve(2, T)
        base = used[0]
        gains = carve(4, HD)
        tab_c, tab_s = carve(TT, HD), carve(TT, HD)
        early_at = [used[0]]
        q_t, k_t = carve(NH, T), carve(NH, T)
        early_at.append(used[0])
        v_s = carve(TT, 512)
        qi_t = carve(4, T)
        ki_t = carve(T)
        o1 = carve(TT, D)
        early_at += [used[0], used[0] + UNIT]
        sig = carve(TT, 2, D)
        early_at.append(used[0])
        gt = carve(2, D)
        b_row = arena[:, 0:D]
        acc = carve(2, 512)
        pq = carve(TT, 512)
        early_at.append(used[0])
        ro = carve(TT, 512)
        score = carve(TT, T)
        mask_d = carve(TT, T)
        kiw = carve(TT, 72)
        kid = carve(TT, P)
        wi = carve(TT, IH)
        rl = carve(2, T)
        early = [v.rearrange("p (k n) -> p k n", k=4) for v in
                 (arena[:, at:at + UNIT] for at in early_at)]
        hf = pq
        rope_a, rope_b = glu_s[:, :, :].rearrange("p a b -> p (a b)"), glu_a[:, :, :].rearrange("p a b -> p (a b)")
        used[0] = base
        v_t = carve(KT, 2 + T)
        cv_t = carve(KT, T)
        y_t = carve(KT, T)
        b_s = carve(TT, D)
        used[0] = base
        kv_d_flat = carve(2048)
        kv_d = kv_d_flat.rearrange("p (t s g u d) -> p t s g u d", t=TT, s=2, g=NG, u=2)
        x2 = carve(2, NG, T)
        kg = carve(3, DH)
        kgb = carve(4, DH)
        kn_t = carve(2, NG, T)
        vn_s = carve(2, TT, 256)
        kd = carve(TT, NG, 2, DH)
        kp = carve(TT, 256)
        xpf = carve(16, 60)
        w2 = carve(2, 2, DH)
        b1r = carve(2, 256)
        hc = carve(256)
        hc_t = carve(2, 60)
        hc_p = carve(2, NG, 4, 32)
        kc = carve(2, DH)
        kc_t = carve(60)
        v_bd = carve(NG, 256)
        gn = carve(TT, 48)
        q_n = carve(8, T)
        pqn = kv_d_flat[:, 0:1024].rearrange("p (t n) -> p t n", t=TT)
        o2 = carve(TT, D)
        pc_s = carve(16, 16)
        pc = carve(NQ, 32)
        pc_t = kp.rearrange("p a b -> p (a b)").rearrange("p (g q) -> p g q", g=NG)
        small = carve(64)

        ident = const[:, C_ID:C_ID + P]
        ones = const[:, C_ONE:C_ONE + P]

        bank = [ctx.enter_context(nc.psum_tensor(f"bank{b}", [P, 512], F32)) for b in range(8)]

        def mask_of(item):
            if item["b"] == "dsa":
                return mask_d[:, item["tt"], 0:P * (item["tt"] + 1)]
            return const[:, C_MASK + P * (1 - item["tt"]):C_MASK + 2 * P]

        def wait_group(eng, tg):
            eng.wait_ge(sem(f"t_free{tg % 2}"), tg // 2 + 1)

        def wait_bank(eng, tg):
            if tg >= 2:
                eng.wait_ge(sem(f"t_free{tg % 2}"), tg // 2)

        def wait_pair(eng, pi):
            eng.wait_ge(sem(f"pair_free{pi % 2}"), pair_after[pi])

        def wait_product(eng, stage, chunk):
            eng.wait_ge(sem("unit_used"), find["unit", stage, chunk] + 1)

        xu = {}
        for n, u in enumerate((0, 1, 2, 3, 4, 5, 5, 6, 7)):
            xu[n] = u

        def unit_view(ring, u, shape):
            v = ring[:, u % RING, 0:int(np.prod(shape))]
            names = "abc"[:len(shape)]
            return v.rearrange(f"p ({' '.join(names)}) -> p {' '.join(names)}",
                               **{k: s for k, s in zip(names[1:], shape[1:])})

        def unit_size(u):
            return unit_source(u)[1]

        class Tick:

            def __init__(self, eng, name):
                self.eng, self.sem, self.count = eng, sem(name), 0

            def __call__(self, ins):
                ins.then_inc(self.sem, 1)
                self.count += 1
                return self.count

            def wait(self, n=None):
                self.eng.wait_ge(self.sem, self.count if n is None else n)

            def step(self, ins):
                self(ins)
                self.wait()

        def ffn_loop():
            return 3, 3

        def mod_half(eng, tick, item):
            m, hh, r = item["m"], item["half"], item["raw"]
            if r < EARLY:
                eng.wait_ge(sem(f"early_full{r}"), 16)
            else:
                eng.wait_ge(sem(f"raw_full{r % RING}"), 32 * turn(r))
            if item["of"] == 0:
                eng.wait_ge(sem("c_ready"), 1)
            if hh == 0 and m >= 3:
                eng.wait_ge(sem("t_done"), find["tg", "mod", m - 2] + 1)
            wv = early[r] if r < EARLY else raw[:, r % RING, :].rearrange("p (k n) -> p k n", k=4)
            a = acc[:, m % 2, :]
            used = sem("mod_used_" + item["by"])
            if item["by"] == "pool":
                tick.step(eng.tensor_tensor(wv, wv, c_act[:, 4 * hh:4 * hh + 4].unsqueeze(2).to_broadcast([P, 4, 512]), ALU.mult))
                tick.step(eng.tensor_tensor(wv[:, 0:2, :], wv[:, 0:2, :], wv[:, 2:4, :], ALU.add))
                if hh == 0:
                    eng.tensor_tensor(a, wv[:, 0, :], wv[:, 1, :], ALU.add).then_inc(used, 1)
                else:
                    tick.step(eng.tensor_tensor(wv[:, 0, :], wv[:, 0, :], wv[:, 1, :], ALU.add))
                    eng.tensor_tensor(a, a, wv[:, 0, :], ALU.add).then_inc(used, 1)
                eng.wait_ge(used, item["of"] + 1)
                return
            for kk in range(4):
                kt = 4 * hh + kk
                if kt == 0:
                    ins = eng.tensor_scalar(a, wv[:, kk, :], c_act[:, 0:1], None, ALU.mult)
                else:
                    ins = eng.scalar_tensor_tensor(a, wv[:, kk, :], c_act[:, kt:kt + 1], a, ALU.mult, ALU.add)
                if kk < 3:
                    tick.step(ins)
                else:
                    ins.then_inc(used, 1)
                    eng.wait_ge(used, item["of"] + 1)

        block = ctx.enter_context(nc.Block())

        @block.sync
        def _(sp):
            def fill(slot, words, src):
                v, full = raw[:, slot, 0:words], sem(f"raw_full{slot}")
                if len(src.shape) == 3:
                    sp.dma_start(v.rearrange("p (k n) -> p k n", k=src.shape[1]), src).then_inc(full, 32)
                    return
                v = v.rearrange("p (k s n) -> p k s n", k=src.shape[1], s=2)
                for half_ in range(2):
                    sp.dma_start(v[:, :, half_, :], src[:, :, half_, :]).then_inc(full, 16)

            sp.dma_start(const[:, 0:C_COSH], A["const"][:, 0:C_COSH]).then_inc(sem("const_full"), 16)
            sp.dma_start(rows2[0:8, :], A["c"].rearrange("a (r q) -> (a r) q", q=P)).then_inc(sem("c_full"), 16)
            sp.dma_start(rows2[8:56, :], A["b_mod"].rearrange("a (r q) -> (a r) q", q=P)).then_inc(sem("c_full"), 16)

            loops = {}
            for item in plan:
                if item["kind"] == "ffn":
                    first, turns = ffn_loop()
                    u0 = item["unit"] + 2 + 3 * (first - 1) + RING
                    loops[unit_raw[u0]] = (item, first, turns)
            r = 0
            while r < len(raws):
                if r in loops:
                    item, first, turns = loops[r]
                    f = item["f"]
                    gu = gate_up[f].rearrange("p k (s n) -> p k s n", s=2)
                    with sp.Fori(0, turns) as i:
                        for h in range(2):
                            for q in range(3):
                                rr = r + 3 * h + q
                                sp.wait_ge(sem("raw_done"), raws[rr - RING][1] + 1 + i * 6)
                                slot = rr % RING
                                if q < 2:
                                    at = (i * 2 + (first + 1 + h)) * GC
                                    src = gu[:, 4 * q:4 * q + 4, :, bass.ds(at, GC)]
                                else:
                                    src = down[f][:, bass.ds((i * 2 + (first + h)) * 2, 2), :]
                                fill(slot, UNIT, src)
                    r += 6 * turns
                    continue
                if r < EARLY:
                    _, m, hf_, _, _ = raws[r]
                    sp.dma_start(early[r], w_mod[:, 4 * hf_:4 * hf_ + 4, 512 * m:512 * m + 512]).then_inc(sem(f"early_full{r}"), 16)
                    r += 1
                    if r == 2:
                        r1 = [A["g_mix_norm"], A["g_ffn_norm"], A["ffn_norm_2"], A["mix_norm_2"], A["kv_norm_2"], A["conv_w_2"], A["cmp_pos_2"]]
                        at = 0
                        for a in r1:
                            n = int(np.prod(a.shape)) // P
                            flat = a if len(a.shape) == 1 else (a.rearrange("a b -> (a b)") if len(a.shape) == 2 else a.rearrange("a b c -> (a b c)"))
                            sp.dma_start(rows1[at:at + n, :], flat.rearrange("(r q) -> r q", q=P)).then_inc(sem("rows_full"), 16)
                            at += n
                        assert at == P
                    continue
                if r >= RING + EARLY:
                    name, value = freed[r - RING]
                    sp.wait_ge(sem(name), value)
                if raws[r][0] == "mod":
                    _, m, hf_, _, _ = raws[r]
                    src, words = w_mod[:, 4 * hf_:4 * hf_ + 4, 512 * m:512 * m + 512], UNIT
                else:
                    src, words = unit_source(raws[r][1])
                fill(r % RING, words, src)
                r += 1
            for tt in range(TT):
                sp.wait_ge(sem("x_ready"), 4 * 8)
                sp.dma_start(out.rearrange("(t p) d -> p t d", p=P)[:, tt, :], x[:, tt, :]).then_inc(sem("stored"), 16)
            sp.wait_ge(sem("stored"), 16 * TT)

        @block.gpsimd
        def _(pool):
            tick = Tick(pool, "pool_tick")

            def inverse_root(dst, src, width, scale, done):
                tick.step(pool.tensor_scalar(src, src, 1.0 / width, EPS, ALU.mult, ALU.add))
                n = dst.free_size() if callable(dst.free_size) else dst.free_size
                hv = half[0:dst.shape[0], 0:n]
                if len(dst.shape) == 3:
                    hv = hv.rearrange("p (a b) -> p a b", a=dst.shape[1])
                ins = pool.tensor_tensor(dst, src, hv, ALU.pow)
                if scale != 1.0:
                    tick.step(ins)
                    ins = pool.tensor_scalar(dst, dst, scale, None, ALU.mult)
                ins.then_inc(sem(done), 1)

            tick.step(pool.memset(half[:, :], -0.5))
            for item in plan:
                k = item["kind"]
                if k == "mod" and item["by"] == "pool":
                    mod_half(pool, tick, item)
                if k == "square":
                    pool.wait_ge(sem("ss_ready"), item["n"] + 1)
                    inverse_root(rstd[:, :], ss[:, :], D, 1.0, "rstd_ready")
                if k == "evac" and item["stage"] in ("qb", "kb", "qa", "ka"):
                    pool.wait_ge(sem("qss_ready"), item["nq"] + 1)
                    if item["stage"][0] == "q":
                        dst = rq[:, 0 if item["stage"] == "qa" else 1, :, :]
                        inverse_root(dst, qss[:, :, 0:NH], HD, -HD ** -0.5, "qr_ready")
                    else:
                        inverse_root(qr[:, :, 0:NH], qss[:, :, 0:NH], HD, 1.0, "qr_ready")
                if k == "evac" and item["stage"] == "kv" and item["chunk"]:
                    pool.wait_ge(sem("qss_ready"), item["nq"] + 1)
                    inverse_root(qr[:, :, 0:NG], qss[:, :, 0:NG], DH, 1.0, "qr_ready")
                if k == "evac" and item["stage"] == "qg":
                    pool.wait_ge(sem("qss_ready"), item["nq"] + 1)
                    c = item["chunk"]
                    inverse_root(rqn[:, :, 8 * c:8 * c + 8], qss[:, :, :], DH, -DH ** -0.5, "qr_ready")
                if k == "cmp" and item["s"] == 0:
                    pool.wait_ge(sem("qss_ready"), item["nq"] + 1)
                    inverse_root(qr[0:60, 0, 0:1], qss[0:60, 0, 0:1], DH, 1.0, "qr_ready")
                if k == "lin" and item["stage"] == "kv" and item["chunk"] == 0 and item["part"] == 0:
                    pool.wait_ge(sem("x_ready"), 4 * xu[5])
                    pool.dma_start(kgb[:, 0:3, :], A["k_norm_2"].rearrange("(o a) b -> o a b", o=1).to_broadcast([P, 3, DH])).then_inc(sem("small_full"), 16)
                    pool.dma_start(kgb[:, 3, :], A["q_norm_2"].to_broadcast([P, DH])).then_inc(sem("small_full"), 16)
                    pool.dma_start(w2, A["cmp_w2_2"].rearrange("s (k p) d -> p s k d", p=P)).then_inc(sem("small_full"), 16)
                    pool.dma_start(b1r[0:1], A["cmp_b1_2"].rearrange("(o s) n -> o s n", o=1)).then_inc(sem("small_full"), 16)
                    pool.memset(v_bd, 0.0)
                    pool.memset(pc, 0.0)
                    pool.memset(hc_p, 0.0).then_inc(sem("zeros_ready"), 1)

        @block.scalar
        def _(act):
            tick = Tick(act, "act_tick")
            act.dma_start(x[:, :, :], A["x"][0].rearrange("(t p) d -> p t d", p=P)).then_inc(sem("x_full"), 16)
            def split(u, r, gate):
                act.wait_ge(sem(f"raw_full{r % RING}"), 32 * turn(r))
                if gate is not None:
                    act.wait_ge(sem("unit_used"), gate)
                words = unit_size(u)
                act.activation(w_hi[:, u % RING, 0:words], raw[:, r % RING, 0:words], ACT.Copy)\
                   .then_inc(sem("hi_ready"), 1)

            for item in plan:
                k = item["kind"]
                if k == "init":
                    act.wait_ge(sem("c_t_done"), 1)
                    act.activation(c_act[:, :], bank[5][:, 0:KT], ACT.Silu).then_inc(sem("c_ready"), 1)
                    for i, g in enumerate(("g_q_dsa", "g_k_dsa", "g_q_moba", "g_k_moba")):
                        act.dma_start(gains[:, i, :], A[g].to_broadcast([P, HD])).then_inc(sem("gains_full"), 16)
                    act.dma_start(b_row[0:1, :], A["b_mod"][0:1, 2 * D:3 * D]).then_inc(sem("b_row_full"), 16)
                    act.dma_start(const[:, C_COSH:], A["const"][:, C_COSH:]).then_inc(sem("tables_full"), 16)
                if k == "split":
                    u = item["unit"]
                    split(u, unit_raw[u], u - RING + 1 if u >= RING else None)
                if k == "square":
                    n = item["n"]
                    if n == 0:
                        act.wait_ge(sem("x_full"), 16)
                    else:
                        act.wait_ge(sem("x_ready"), 4 * xu[n])
                        act.wait_ge(sem("rstd_ready"), n)
                    for tt in range(TT):
                        ins = act.activation(junk[:, :], x[:, tt, :], ACT.Square, accum_out=ss[:, tt:tt + 1])
                        tick.step(ins) if tt < TT - 1 else ins.then_inc(sem("ss_ready"), 1)
                if k == "tp":
                    st, tg, g = item["stage"], item["tg"], item["g"]
                    b = bank[6 + tg % 2]
                    if st in PAIRED or st in ("qi", "qb", "kb", "qa", "ka", "ki", "kvt", "qn", "hc", "kc", "pc") or \
                            (st == "p" and item["it"] % 2 == 0):
                        act.wait_ge(sem("t_done"), tg + 1)
                    free = sem(f"t_free{tg % 2}")
                    if st == "norm":
                        col = {2: 16, 3: 48, 4: 24, 5: 64, 6: 32, 7: 56, 8: 40}[item["norm"]]
                        for kk in range(2):
                            ins = act.activation(h_hi[:, 2 * g + kk, :], b[:, kk * T:(kk + 1) * T], ACT.Copy,
                                                 scale=cols1[:, col + 2 * g + kk:col + 2 * g + kk + 1])
                        ins.then_inc(sem("hi_t"), 1)
                    elif st == "normf":
                        n = item["norm"]
                        if g == 0:
                            act.wait_ge(sem("mod_ready"), n + 1)
                        for kk in range(2):
                            c = 2 * g + kk
                            ins = act.activation(hf[:, kk, T * (g % 2):T * (g % 2) + T], b[:, kk * T:(kk + 1) * T], ACT.Identity,
                                                 scale=mod_s[:, n, c:c + 1], bias=modc[:, n, c:c + 1])
                        ins.then_inc(sem("hi_t"), 1)
                    elif st in ("o", "merged", "on"):
                        kt = 2 * g
                        act.activation(h_hi[:, kt:kt + 2, :].rearrange("p a b -> p (a b)"), b[:, :], ACT.Copy)\
                           .then_inc(sem("hi_t"), 1)
                    elif st in ("qb", "kb", "qa", "ka"):
                        dst = (q_t if st[0] == "q" else k_t)[:, 2 * g:2 * g + 2, :].rearrange("p a b -> p (a b)")
                        act.activation(dst, b[:, :], ACT.Copy).then_inc(free, 1)
                    elif st == "qi":
                        act.activation(qi_t[:, 2 * g:2 * g + 2, :].rearrange("p a b -> p (a b)"), b[:, :], ACT.Copy)\
                           .then_inc(free, 1)
                    elif st == "ki":
                        act.activation(ki_t, b[:, 0:T], ACT.Copy).then_inc(free, 1)
                    elif st == "kvt" and item["c"] == 0:
                        s_, g0 = divmod(2 * g, NG)
                        bv = b[:, :].rearrange("p (a t) -> p a t", a=2)
                        act.activation(x2[0:64, s_, g0:g0 + 2, :], bv[0:64], ACT.Copy)
                        act.activation(x2[64:128, s_, g0:g0 + 2, 0:T - 1], bv[64:128, :, 1:T], ACT.Copy)\
                           .then_inc(free, 1)
                    elif st == "kvt":
                        act.activation(kn_t[:, item["c"] - 1, 2 * g:2 * g + 2, :].rearrange("p a b -> p (a b)"),
                                       b[:, :], ACT.Copy).then_inc(free, 1)
                    elif st == "qn":
                        m = 4 * item["c"] + 2 * g
                        act.activation(q_n[:, m:m + 2, :].rearrange("p a b -> p (a b)"), b[:, :], ACT.Copy)\
                           .then_inc(free, 1)
                    elif st == "hc":
                        act.wait_ge(sem("zeros_ready"), 1)
                        bv = b[:, 0:120].rearrange("p (k c) -> p k c", k=2)
                        if item["c"] == 0:
                            act.activation(hc_t, bv, ACT.Copy).then_inc(free, 1)
                        else:
                            for kk in range(2):
                                for hh in range(4):
                                    ins = act.activation(hc_p[:, kk, :, hh, 0:NC],
                                                         bv[:, kk, :].rearrange("p (g n) -> p g n", g=NG), ACT.Copy)
                            ins.then_inc(free, 1)
                    elif st == "kc":
                        act.activation(kc_t, b[:, 0:60], ACT.Copy).then_inc(free, 1)
                    elif st == "pc":
                        act.activation(pc_t.rearrange("p a b -> p (a b)"), b[:, :], ACT.Copy).then_inc(free, 1)
                    elif st == "p" and item["it"] % 2 == 0:
                        n = P * (item["tt"] + 1)
                        act.activation(pt_s[:, item["it"] % 2, 0:n], b[:, 0:n], ACT.Copy).then_inc(free, 1)
                if k == "evac":
                    st, c, pi = item["stage"], item["chunk"], item["pi"]
                    b = [bank[2 * (pi % 2) + tt] for tt in range(TT)]
                    free = sem(f"pair_free{pi % 2}")
                    if st not in ("ba", "bb", "out1", "co", "wo"):
                        wait_product(act, st, c)
                    if st in ("qi", "qb", "kb", "qa", "ka"):
                        if item["rope"]:
                            act.wait_ge(sem("rope_done"), item["rope"])
                        for tt in range(TT):
                            ins = act.activation(pq[:, tt, :], b[tt][:, :], ACT.Copy)
                        if st != "qi":
                            for tt in range(TT):
                                ins = act.activation(junk[:, tt * 512:(tt + 1) * 512], b[tt][:, :], ACT.Square)
                        ins.then_inc(free, 1)
                    elif st == "ki":
                        for tt in range(TT):
                            ins = act.activation(kiw[:, tt, :], b[tt][:, 0:72], ACT.Copy)
                        ins.then_inc(free, 1)
                    elif st in ("va", "vb"):
                        if st == "va":
                            act.wait_ge(sem("pv_done"), 8)
                        for tt in range(TT):
                            ins = act.activation(v_s[:, tt, :], b[tt][:, :], ACT.Copy)
                        ins.then_inc(free, 1)
                    elif st in ("ga", "gb"):
                        for tt in range(TT):
                            ins = act.activation(sig[:, tt, 0 if st == "ga" else 1, 512 * c:512 * c + 512], b[tt][:, :], ACT.Copy)
                        ins.then_inc(free, 1)
                    elif st == "cb":
                        for tt in range(TT):
                            ins = act.activation(b_s[:, tt, 512 * c:512 * c + 512], b[tt][:, :], ACT.Copy, scale=rstd[:, tt:tt + 1])
                        ins.then_inc(free, 1)
                    elif st == "kv" and c == 0:
                        act.wait_ge(sem("rstd_ready"), 6)
                        for tt in range(TT):
                            for s_ in range(2):
                                for dup in range(2):
                                    ins = act.activation(kv_d[:, tt, s_, :, dup, :],
                                                         b[tt][:, 256 * s_:256 * s_ + 256].rearrange("p (g d) -> p g d", g=NG),
                                                         ACT.Copy, scale=rstd[:, tt:tt + 1])
                        ins.then_inc(free, 1)
                    elif st == "kv":
                        if c == 2:
                            act.wait_ge(sem("kd_done"), 1)
                        for tt in range(TT):
                            act.activation(kp[:, tt, :], b[tt][:, 0:256], ACT.Copy, scale=rstd[:, tt:tt + 1])
                            act.activation(junk[:, tt * 256:(tt + 1) * 256], b[tt][:, 0:256], ACT.Square, scale=rstd[:, tt:tt + 1])
                            ins = act.activation(vn_s[:, c - 1, tt, :], b[tt][:, 256:512], ACT.Copy, scale=rstd[:, tt:tt + 1])
                        ins.then_inc(free, 1)
                    elif st == "cm":
                        act.activation(hc[0:60], b[0][0:60, 0:256], ACT.Gelu_apprx_tanh).then_inc(free, 1)
                    elif st == "gn":
                        act.wait_ge(sem("rstd_ready"), 8)
                        for tt in range(TT):
                            ins = act.activation(gn[:, tt, :], b[tt][:, 0:48], ACT.Sigmoid, scale=rstd[:, tt:tt + 1])
                        ins.then_inc(free, 1)
                    elif st == "qg":
                        act.wait_ge(sem("rstd_ready"), 8)
                        if c:
                            act.wait_ge(sem("qss_ready"), item["nq"])
                            act.wait_ge(sem("t_done"), find["tg", "qn", (0, 1)] + 1)
                        for tt in range(TT):
                            act.activation(pqn[:, tt, :], b[tt][:, :], ACT.Copy, scale=rstd[:, tt:tt + 1])
                            ins = act.activation(junk[:, tt * 512:(tt + 1) * 512], b[tt][:, :], ACT.Square, scale=rstd[:, tt:tt + 1])
                        ins.then_inc(free, 1)
                if k == "ix":
                    act.wait_ge(sem("ix_done"), item["n"] + 1)
                    for hh in range(2):
                        n = P * (item["tt"] + 1)
                        if item["n"]:
                            act.wait_ge(sem("ix_used"), 2 * item["n"] - 1 + hh)
                        act.activation(rl[:, hh, 0:n], bank[4 + hh][:, 0:n], ACT.Relu).then_inc(sem("rl_ready"), 1)
                if k == "sm":
                    it = item["it"]
                    n = P * (item["tt"] + 1)
                    act.wait_ge(sem("sm_done"), it + 1)
                    if it >= 2:
                        act.wait_ge(sem("t_done"), find["tg", "p", it - 2] + 1)
                    act.activation(p_s[:, it % 2, 0:n], s_s[:, it % 2, 0:n], ACT.Exp, scale=-1.0,
                                   bias=mn[:, it:it + 1], accum_out=sm[:, it:it + 1]).then_inc(sem("exp_done"), 1)
                if k == "sigmoid":
                    act.wait_ge(sem("o_ready"), 2 * NH * TT)
                    act.dma_start(b_row[0:1, :], A["b_mod"][0:1, 5 * D:6 * D]).then_inc(sem("b_row_full"), 16)
                    for c_ in range(2):
                        wait_pair(act, find["pi", "gb", c_])
                    for tt in range(TT):
                        for a in range(2):
                            ins = act.activation(sig[:, tt, a, :], sig[:, tt, a, :], ACT.Sigmoid)
                    ins.then_inc(sem("sig_ready"), 1)
                if k == "cs":
                    act.wait_ge(sem("cs_ready"), item["tt"] + 1)
                    act.activation(pc_s, pc_s, ACT.Exp, scale=-1.0).then_inc(sem("cs_exp"), 1)
                if k == "co_":
                    act.wait_ge(sem("cv_done"), item["tt"] + 1)
                    for a in range(2):
                        ins = act.activation(o2[:, item["tt"], 512 * a:512 * a + 512], bank[4 + a][:, :], ACT.Copy)
                    ins.then_inc(sem("oc_ready"), 1)
                if k == "xp":
                    act.wait_ge(sem("xp_full"), item["s"] + 1)
                    act.activation(xp_hi[:, :, :].rearrange("p a b -> p (a b)"), xpf.rearrange("p a b -> p (a b)"),
                                   ACT.Copy).then_inc(sem("xp_hi_ready"), 1)
                if k == "glu":
                    if item["j"] == 0:
                        act.wait_ge(sem("rstd_ready"), 4)
                    act.wait_ge(sem("unit_used"), item["unit"] + 2)
                    for tt in range(TT):
                        act.activation(glu_s[:, tt, :], bank[tt][:, 0:GC], ACT.Copy, scale=rstd[:, tt:tt + 1])\
                           .then_inc(sem("sg_ready"), 1)
                    act.wait_ge(sem("t_done"), item["tg"] + 1)
                    act.activation(v_t[:, 2 * item["j"]:2 * item["j"] + 2, 2:2 + T],
                                   bank[6 + item["tg"] % 2][:, :].rearrange("p (a t) -> p a t", a=2), ACT.Copy)\
                       .then_inc(sem(f"t_free{item['tg'] % 2}"), 1)
                if k == "ffn":
                    f = item["f"]
                    if f:
                        act.wait_ge(sem("rstd_ready"), item["norm"] + 1)

                    def step(jb, i=None):
                        two = lambda a: 0 if i is None else a * 2 * i

                        def next_split(q):
                            u = item["unit"] + (2 + 3 * (jb - 1) if jb else 0) + q + RING
                            if u >= len(units) or u < item["have"]:
                                return
                            split_at(u)

                        def split_at(u):
                            act.wait_ge(sem(f"raw_full{unit_raw[u] % RING}"), 32 * turn(unit_raw[u]) + two(32))
                            act.wait_ge(sem("unit_used"), u - RING + 1 + two(3))
                            act.activation(w_hi[:, u % RING, :], raw[:, unit_raw[u] % RING, :], ACT.Copy)\
                               .then_inc(sem("hi_ready"), 1)

                        qs = [0, 1, 2] if jb else [0, 1]
                        if jb < NJ:
                            next_split(0)
                            act.wait_ge(sem("unit_used"), item["unit"] + 3 * jb + (1 if jb else 2) + two(3))
                            for tt in range(TT):
                                act.activation(glu_s[:, tt, :], bank[tt][:, 0:GC], ACT.Silu,
                                               scale=rstd[:, tt:tt + 1] if f else 1.0).then_inc(sem("sg_ready"), 1)
                            if jb < NJ - 1:
                                for q in qs[1:]:
                                    next_split(q)
                            tg = item["tg"] + jb
                            act.wait_ge(sem("t_done"), tg + 1 + two(1))
                            act.activation(f_hi[:, jb % 2, :, :].rearrange("p a b -> p (a b)"), bank[6 + tg % 2][:, :],
                                           ACT.Copy).then_inc(sem("hi_t"), 1)
                            if jb == NJ - 1:
                                for q in qs[1:]:
                                    next_split(q)
                        else:
                            u = item["unit"] + 3 * NJ - 1 + RING
                            if u < len(units):
                                split_at(u)

                    first, turns = ffn_loop()
                    for j in range(first):
                        step(j)
                    with act.Fori(0, turns) as i:
                        for h in range(2):
                            step(first + h, i)
                    for j in range(first + 2 * turns, NJ + 1):
                        step(j)

        @block.vector
        def _(dve):
            tick = Tick(dve, "dve_tick")

            updates, after_norm = [0], []

            def lo_split(u, r, two=lambda a: 0):
                dve.wait_ge(sem("hi_ready"), u + 1 + two(3))
                words = unit_size(u)
                dve.tensor_tensor(w_lo[:, u % RING, 0:words], raw[:, r % RING, 0:words],
                                  w_hi[:, u % RING, 0:words].bitcast(F32), ALU.subtract).then_inc(sem("raw_done"), 1)

            def rope(dst, src, cos, sin, heads, w, done=None):
                n = heads * w
                s3 = src.rearrange("p (h w) -> p h w", h=heads)
                a3 = rope_a[:, 0:n].rearrange("p (h w) -> p h w", h=heads)
                b3 = rope_b[:, 0:n].rearrange("p (h w) -> p h w", h=heads)

                def over(t):
                    return t.unsqueeze(1).to_broadcast([P, heads, t.shape[-1]])

                tick(dve.tensor_tensor(a3, s3, over(cos), ALU.mult))
                tick(dve.tensor_tensor(b3[:, :, 0:w // 2], s3[:, :, w // 2:w], over(sin[:, 0:w // 2]), ALU.mult))
                tick.step(dve.tensor_tensor(b3[:, :, w // 2:w], s3[:, :, 0:w // 2], over(sin[:, w // 2:w]), ALU.mult))
                ins = dve.tensor_tensor(dst, rope_a[:, 0:n], rope_b[:, 0:n], ALU.add)
                tick.step(ins) if done is None else ins.then_inc(sem(done), 1)

            def update(tt, nb, src, how):
                xv = x[:, tt, 512 * nb:512 * nb + 512]
                if how == "half":
                    ins = dve.scalar_tensor_tensor(xv, src, 0.5, xv, ALU.mult, ALU.add)
                elif how == "one":
                    ins = dve.tensor_tensor(xv, src, xv, ALU.add)
                else:
                    g = gt[:, how, 512 * nb:512 * nb + 512]
                    tmp = rope_a if updates[0] % 2 else rope_b
                    if updates[0] >= 2:
                        dve.wait_ge(sem("x_ready"), updates[0] - 1)
                    tick.step(dve.tensor_tensor(tmp, src, g, ALU.mult))
                    ins = dve.tensor_tensor(xv, tmp, xv, ALU.add)
                ins.then_inc(sem("x_ready"), 1)
                updates[0] += 1

            for item in plan:
                k = item["kind"]
                if k in ("square", "xp") and after_norm:
                    u = after_norm.pop()
                    lo_split(u, unit_raw[u])
                if k == "split":
                    lo_split(item["unit"], unit_raw[item["unit"]])
                if k == "mod" and item["by"] == "dve":
                    mod_half(dve, tick, item)
                    if item["m"] == 1 and item["half"] == 1:
                        dve.wait_ge(sem("init_done"), 1)
                        tick(dve.tensor_copy(cols1[:, :], bank[4][:, 0:P]))
                        dve.tensor_copy(cols2[:, :], bank[4][:, P:P + 56]).then_inc(sem("cols_ready"), 1)
                        dve.wait_ge(sem("cols_ready"), 1)
                if k == "mod_a":
                    n = item["norm"]
                    for g in range(6 * n, 6 * n + 4):
                        wait_group(dve, find["tg", "mod", g])
                    dve.scalar_tensor_tensor(mod_s[:, n, :], modc[:, n, 8:16], 1.0, cols1[:, 8 * n:8 * n + 8],
                                             ALU.add, ALU.mult).then_inc(sem("mod_ready"), 1)
                if k == "scale_x":
                    dve.wait_ge(sem("rstd_ready"), item["norm"] + 1)
                    for tt in range(TT):
                        ins = dve.tensor_scalar(o1[:, tt, :], x[:, tt, :], rstd[:, tt:tt + 1], None, ALU.mult)
                        ins.then_inc(sem("xn_ready"), 1)
                if k == "tp":
                    st, tg, g = item["stage"], item["tg"], item["g"]
                    b = bank[6 + tg % 2]
                    free = sem(f"t_free{tg % 2}")
                    if st == "mod":
                        dve.wait_ge(sem("t_done"), tg + 1)
                        which = g // 2
                        if which in (2, 5):
                            dve.tensor_copy(gt[:, which // 3, 512 * (g % 2):512 * (g % 2) + 512], b[:, :]).then_inc(free, 1)
                        else:
                            n, at = (0, which) if which < 2 else (1, which - 3)
                            at = 8 * at + 4 * (g % 2)
                            bc = 8 + 4 * g
                            dve.tensor_tensor(modc[:, n, at:at + 4], b[:, 0:4], cols2[:, bc:bc + 4], ALU.add).then_inc(free, 1)
                    if st in PAIRED:
                        dve.wait_ge(sem("hi_t"), item["hl"] + 1)
                        if st == "norm":
                            col = {2: 16, 3: 48, 4: 24, 5: 64, 6: 32, 7: 56, 8: 40}[item["norm"]]
                            for kk in range(2):
                                c = 2 * g + kk
                                ins = dve.scalar_tensor_tensor(h_lo[:, c, :], b[:, kk * T:(kk + 1) * T], cols1[:, col + c:col + c + 1],
                                                               h_hi[:, c, :].bitcast(F32), ALU.mult, ALU.subtract)
                            ins.then_inc(free, 1)
                        elif st == "normf":
                            hv = h_hi[:, 2 * g:2 * g + 2, :]
                            tick.step(dve.tensor_copy(hv, hf[:, :, T * (g % 2):T * (g % 2) + T]))
                            dve.tensor_tensor(h_lo[:, 2 * g:2 * g + 2, :], hf[:, :, T * (g % 2):T * (g % 2) + T], hv.bitcast(F32), ALU.subtract)\
                               .then_inc(free, 1)
                        else:
                            dve.tensor_tensor(h_lo[:, 2 * g:2 * g + 2, :].rearrange("p a b -> p (a b)"), b[:, :],
                                              h_hi[:, 2 * g:2 * g + 2, :].rearrange("p a b -> p (a b)").bitcast(F32), ALU.subtract)\
                               .then_inc(free, 1)
                    if st == "cb":
                        c0 = 2 * g
                        dve.wait_ge(sem("t_done"), tg + 1)
                        yv = y_t[:, c0:c0 + 2, :].rearrange("p a b -> p (a b)")
                        hv = h_hi[:, c0:c0 + 2, :].rearrange("p a b -> p (a b)")
                        tick.step(dve.tensor_tensor(yv, b[:, :], cv_t[:, c0:c0 + 2, :].rearrange("p a b -> p (a b)"), ALU.mult))
                        tick.step(dve.tensor_copy(hv, yv))
                        dve.tensor_tensor(h_lo[:, c0:c0 + 2, :].rearrange("p a b -> p (a b)"), yv, hv.bitcast(F32), ALU.subtract)\
                           .then_inc(free, 1)
                    if st == "p" and item["it"] % 2:
                        n = P * (item["tt"] + 1)
                        dve.wait_ge(sem("t_done"), tg + 1)
                        dve.tensor_copy(pt_s[:, item["it"] % 2, 0:n], b[:, 0:n]).then_inc(free, 1)
                if k == "conv":
                    wait_group(dve, find["glu tg"])
                    wait_group(dve, find["glu tg"] - 1)
                    dve.wait_ge(sem("v_t_ready"), 1)
                    for kt in (2 * item["g"], 2 * item["g"] + 1):
                        cw = [cols1[:, 72 + 8 * w + kt:73 + 8 * w + kt] for w in range(3)]
                        cv = cv_t[:, kt, :]
                        tick.step(dve.tensor_scalar(cv, v_t[:, kt, 0:T], cw[0], None, ALU.mult))
                        tick.step(dve.scalar_tensor_tensor(cv, v_t[:, kt, 1:1 + T], cw[1], cv, ALU.mult, ALU.add))
                        tick.step(dve.scalar_tensor_tensor(cv, v_t[:, kt, 2:2 + T], cw[2], cv, ALU.mult, ALU.add))
                if k == "evac":
                    st, c, pi = item["stage"], item["chunk"], item["pi"]
                    b = [bank[2 * (pi % 2) + tt] for tt in range(TT)]
                    free = sem(f"pair_free{pi % 2}")
                    if st in ("ba", "bb"):
                        wait_product(dve, st, c)
                        dve.wait_ge(sem("sig_ready"), 1)
                        if st == "bb":
                            wait_pair(dve, find["pi", "ba", c])
                        for tt in range(TT):
                            a = 0 if st == "ba" else 1
                            v = sig[:, tt, a, 512 * c:512 * c + 512]
                            if st == "ba":
                                ins = dve.tensor_tensor(v, b[tt][:, :], v, ALU.mult)
                                ins.then_inc(free, 1) if tt else tick(ins)
                            else:
                                tick.step(dve.tensor_tensor(v, b[tt][:, :], v, ALU.mult))
                                ins = dve.tensor_tensor(sig[:, tt, 0, 512 * c:512 * c + 512],
                                                        sig[:, tt, 0, 512 * c:512 * c + 512], v, ALU.add)
                                ins.then_inc(free, 1) if tt else tick(ins)
                    elif st in ("out1", "co", "wo"):
                        wait_product(dve, st, c)
                        for tt in range(TT):
                            update(tt, c, b[tt][:, :], 0 if st == "out1" else "one")
                    elif st in ("qb", "kb", "qa", "ka"):
                        gi = ("qa", "ka", "qb", "kb").index(st)
                        if item["nq"] == 0:
                            dve.wait_ge(sem("gains_full"), 16 * 4)
                            dve.wait_ge(sem("tables_full"), 16)
                        gv = gains[:, gi, :]
                        for tt in range(TT):
                            cb = const[:, C_COSH + tt * HD:C_COSH + (tt + 1) * HD]
                            sb_ = const[:, C_SINH + tt * HD:C_SINH + (tt + 1) * HD]
                            tick(dve.tensor_tensor(tab_c[:, tt, :], cb, gv, ALU.mult))
                            tick(dve.tensor_tensor(tab_s[:, tt, 0:64], sb_[:, 0:64], gv[:, 64:128], ALU.mult))
                            tick(dve.tensor_tensor(tab_s[:, tt, 64:128], sb_[:, 64:128], gv[:, 0:64], ALU.mult))
                        tick.wait()
                        wait_pair(dve, pi)
                        for tt in range(TT):
                            ins = dve.tensor_reduce(qss[:, tt, 0:NH], junk[:, tt * 512:(tt + 1) * 512].rearrange("p (h w) -> p h w", h=NH),
                                                    AX.X, ALU.add)
                            tick(ins) if tt == 0 else ins.then_inc(sem("qss_ready"), 1)
                        before = {"qb": "qi", "kb": "qb", "qa": "kb", "ka": "qa"}[st]
                        dve.wait_ge(sem("t_done"), find["tg", before, 1] + 1)
                        for tt in range(TT):
                            rope(ro[:, tt, :], pq[:, tt, :], tab_c[:, tt, :], tab_s[:, tt, :], NH, HD,
                                 "rope_done" if st[0] == "q" and tt else None)
                        dve.wait_ge(sem("qr_ready"), item["nq"] + 1)
                        if st[0] == "k":
                            for tt in range(TT):
                                rv = ro[:, tt, :].rearrange("p (h w) -> p h w", h=NH)
                                ins = dve.tensor_tensor(rv, rv, qr[:, tt, 0:NH].unsqueeze(2).to_broadcast([P, NH, HD]), ALU.mult)
                                ins.then_inc(sem("rope_done"), 1) if tt else tick(ins)
                    elif st == "qi":
                        wait_pair(dve, pi)
                        for tt in range(TT):
                            rope(ro[:, tt, :], pq[:, tt, :], const[:, C_COSI + tt * ID:C_COSI + (tt + 1) * ID],
                                 const[:, C_SINI + tt * ID:C_SINI + (tt + 1) * ID], IH, ID, "rope_done" if tt else None)
                    elif st == "ki":
                        wait_pair(dve, pi)
                        dve.wait_ge(sem("tables_full"), 16)
                        for tt in range(TT):
                            tick.step(dve.tensor_scalar(wi[:, tt, :], kiw[:, tt, ID:ID + IH], HI_SCALE, None, ALU.mult))
                            rope(kid[:, tt, 0:ID], kiw[:, tt, 0:ID], const[:, C_COSI + tt * ID:C_COSI + (tt + 1) * ID],
                                 const[:, C_SINI + tt * ID:C_SINI + (tt + 1) * ID], 1, ID)
                            ins = dve.tensor_copy(kid[:, tt, ID:2 * ID], kid[:, tt, 0:ID])
                            ins.then_inc(sem("kid_ready"), 1) if tt else tick(ins)
                    elif st == "kv" and c:
                        wait_pair(dve, pi)
                        if c == 1:
                            dve.wait_ge(sem("small_full"), 16 * 4)
                            tick.step(dve.tensor_tensor(kg, kgb[:, 0:3, :], kgb[:, 3, :].unsqueeze(1).to_broadcast([P, 3, DH]), ALU.mult))
                        for tt in range(TT):
                            ins = dve.tensor_reduce(qss[:, tt, 0:NG], junk[:, tt * 256:(tt + 1) * 256].rearrange("p (h w) -> p h w", h=NG),
                                                    AX.X, ALU.add)
                            tick(ins) if tt == 0 else ins.then_inc(sem("qss_ready"), 1)
                        dve.wait_ge(sem("qr_ready"), item["nq"] + 1)
                        if c == 2:
                            dve.wait_ge(sem("t_done"), find["tg", "kvt", (1, 1)] + 1)
                        for tt in range(TT):
                            kv3 = kp[:, tt, :].rearrange("p (g w) -> p g w", g=NG)
                            tick.step(dve.tensor_tensor(kv3, kv3, qr[:, tt, 0:NG].unsqueeze(2).to_broadcast([P, NG, DH]), ALU.mult))
                            for dup in range(2):
                                ins = dve.tensor_tensor(kd[:, tt, :, dup, :], kv3, kg[:, c, :].unsqueeze(1).to_broadcast([P, NG, DH]), ALU.mult)
                                ins.then_inc(sem("kd_done"), 1) if tt and dup else tick(ins)
                    elif st == "qg":
                        wait_pair(dve, pi)
                        for tt in range(TT):
                            ins = dve.tensor_reduce(qss[:, tt, :], junk[:, tt * 512:(tt + 1) * 512].rearrange("p (h w) -> p h w", h=8),
                                                    AX.X, ALU.add)
                            tick(ins) if tt == 0 else ins.then_inc(sem("qss_ready"), 1)
                        dve.wait_ge(sem("qr_ready"), item["nq"] + 1)
                if k == "ix":
                    n = P * (item["tt"] + 1)
                    for hh in range(2):
                        h = 2 * item["pair"] + hh
                        sc = score[:, item["tt"], 0:n]
                        dve.wait_ge(sem("rl_ready"), 2 * item["n"] + hh + 1)
                        if h:
                            dve.wait_ge(sem("ix_used"), 2 * item["n"] + hh)
                        prev = const[:, C_MASK + P * (1 - item["tt"]):C_MASK + 2 * P] if h == 0 else sc
                        dve.scalar_tensor_tensor(sc, rl[:, hh, 0:n], wi[:, item["tt"], h:h + 1], prev, ALU.mult, ALU.add)\
                           .then_inc(sem("ix_used"), 1)
                if k == "topk":
                    tt = item["tt"]
                    n = P * (tt + 1)
                    sc = score[:, tt, 0:n]
                    dve.wait_ge(sem("ix_used"), 8 * (tt + 1))
                    for _ in range(TOPK // 8 // 4):
                        tick.step(dve.max(top8[:, :], sc))
                        tick.step(dve.match_replace(sc, top8[:, :], sc, TAKEN))
                    if item["piece"] < 3:
                        continue
                    tick.step(dve.tensor_scalar(mask_d[:, tt, 0:n], sc, -2e38, NEG, ALU.is_gt, ALU.mult))
                    tick.step(dve.tensor_tensor(mask_d[:, tt, 0:n], mask_d[:, tt, 0:n],
                                                const[:, C_MASK + P * (1 - tt):C_MASK + 2 * P], ALU.add))
                if k == "sm":
                    it, tt = item["it"], item["tt"]
                    n = P * (tt + 1)
                    dve.wait_ge(sem("qk_done"), it + 1)
                    if it >= 2:
                        dve.wait_ge(sem("exp_done"), it - 1)
                    if item["b"] in ("dsa", "moba"):
                        scale = rq[:, 0 if item["b"] == "dsa" else 1, tt, item["h"]:item["h"] + 1]
                    else:
                        scale = rqn[:, tt, item["h"]:item["h"] + 1]
                    dve.tensor_tensor_reduce(s_s[:, it % 2, 0:n], bank[4 + it % 2][:, 0:n], mask_of(item), scale, 3e38,
                                             ALU.add, ALU.min, mn[:, it:it + 1]).then_inc(sem("sm_done"), 1)
                if k == "pv":
                    it, tt, h = item["it"], item["tt"], item["h"]
                    tick.step(dve.reciprocal(rc[:, it:it + 1], sm[:, it:it + 1]))
                    dve.wait_ge(sem("pv_done"), it + 1)
                    if item["b"] in ("dsa", "moba"):
                        at = 512 * (item["b"] == "moba") + HD * h
                        dve.tensor_scalar(o1[:, tt, at:at + HD], bank[6 + find["tg", "p", it] % 2][:, T:T + HD], rc[:, it:it + 1], None, ALU.mult)\
                           .then_inc(sem("o_ready"), 1)
                    else:
                        j = 1 + (item["b"] == "win")
                        if item["b"] == "sel" and it == 16:
                            dve.wait_ge(sem("oc_ready"), 2)
                        gcol = gn[:, tt, 3 * h + j:3 * h + j + 1]
                        tick.step(dve.tensor_tensor(rc[:, it:it + 1], rc[:, it:it + 1], gcol, ALU.mult))
                        ov = o2[:, tt, DH * h:DH * h + DH]
                        dve.scalar_tensor_tensor(ov, bank[6 + find["tg", "p", it] % 2][:, T:T + DH], rc[:, it:it + 1], ov, ALU.mult, ALU.add)\
                           .then_inc(sem("o_ready"), 1)
                if k == "cs":
                    tt = item["tt"]
                    dve.wait_ge(sem("cs_done"), tt + 1)
                    if tt:
                        dve.wait_ge(sem("t_done"), find["tg", "pc", (0, 0)] + 1)
                    pv = pc_s.rearrange("p (m e) n -> p m e n", e=2)
                    for e in range(2):
                        r_ = rqn[:, tt, :].rearrange("p (m e) -> p m e", e=2)[:, :, e].unsqueeze(2).to_broadcast([P, 8, NC])
                        src = bank[4 + e][:, 0:128].rearrange("p (m n) -> p m n", n=16)[:, :, 0:NC]
                        tick(dve.tensor_tensor(pv[:, :, e, 0:NC], src, r_, ALU.mult))
                    tick.wait()
                    v = pc_s[:, :, 0:NC]
                    cm = const[:, C_CM + 16 * tt:C_CM + 16 * tt + NC].unsqueeze(1).to_broadcast([P, NQ, NC])
                    cv = const[:, C_CV + 16 * tt:C_CV + 16 * tt + NC].unsqueeze(1).to_broadcast([P, NQ, NC])
                    tick.step(dve.tensor_tensor(v, v, cm, ALU.add))
                    tick.step(dve.tensor_reduce(small[:, 0:NQ], v, AX.X, ALU.min))
                    tick.step(dve.memset(pc_s[:, :, NC:16], 0.0))
                    dve.tensor_tensor(v, v, small[:, 0:NQ].unsqueeze(2).to_broadcast([P, NQ, NC]), ALU.subtract)\
                       .then_inc(sem("cs_ready"), 1)
                    dve.wait_ge(sem("cs_exp"), tt + 1)
                    tick.step(dve.tensor_reduce(small[:, 16:32], v, AX.X, ALU.add))
                    tick.step(dve.reciprocal(small[:, 32:48], small[:, 16:32]))
                    g0 = gn[:, tt, :].rearrange("p (h j) -> p h j", j=3)[:, :, 0]
                    tick.step(dve.tensor_tensor(small[:, 32:48], small[:, 32:48], g0, ALU.mult))
                    tick.step(dve.tensor_tensor(v, v, cv, ALU.mult))
                    if tt == 0:
                        dve.wait_ge(sem("zeros_ready"), 1)
                    dve.tensor_tensor(pc[:, :, 0:NC], v, small[:, 32:48].unsqueeze(2).to_broadcast([P, NQ, NC]), ALU.mult)\
                       .then_inc(sem("pc_ready"), 1)
                if k == "xp":
                    s_ = item["s"]
                    if s_ == 0:
                        wait_group(dve, find["tg", "kvt", (0, 2)])
                        wait_group(dve, find["tg", "kvt", (0, 3)])
                    else:
                        dve.wait_ge(sem("xp_hi_ready"), 1)
                        wait_product(dve, "cm", 0)
                    pos = cols1[:, 96 + 16 * s_:96 + 16 * s_ + 16]
                    for g in range(NG):
                        xv = x2[:, s_, g, :].rearrange("p (n a) -> p n a", a=CS)
                        for e in range(2):
                            dst = xpf[:, 8 * e:8 * e + 8, NC * g:NC * g + NC].rearrange("p k n -> p n k")
                            ins = dve.tensor_tensor(dst, xv[:, e:e + NC, 0:CS:2],
                                                    pos[:, 8 * e:8 * e + 8].unsqueeze(1).to_broadcast([P, NC, 8]), ALU.add)
                            ins.then_inc(sem("xp_full"), 1) if g == NG - 1 and e else tick(ins)
                    dve.wait_ge(sem("xp_hi_ready"), s_ + 1)
                    dve.tensor_tensor(xp_lo[:, :, :].rearrange("p a b -> p (a b)"), xpf.rearrange("p a b -> p (a b)"),
                                      xp_hi[:, :, :].rearrange("p a b -> p (a b)").bitcast(F32), ALU.subtract)\
                       .then_inc(sem("xp_ready"), 1)
                if k == "cmp":
                    dve.wait_ge(sem("cmp_done"), item["s"] + 1)
                    if item["s"] == 0:
                        kcv = bank[4][0:60, 0:DH]
                        tick.step(dve.tensor_copy(kc[0:60, 0, :], kcv))
                        tick.step(dve.tensor_tensor(kc[0:60, 1, :], kc[0:60, 0, :], kc[0:60, 0, :], ALU.mult))
                        dve.tensor_reduce(qss[0:60, 0, 0:1], kc[0:60, 1, :], AX.X, ALU.add).then_inc(sem("qss_ready"), 1)
                        dve.wait_ge(sem("qr_ready"), item["nq"] + 1)
                        tick.step(dve.scalar_tensor_tensor(kc[0:60, 0, :], kc[0:60, 0, :], qr[0:60, 0, 0:1], kg[0:60, 0, :], ALU.mult, ALU.mult))
                        dve.tensor_copy(kc[0:60, 1, :], kc[0:60, 0, :]).then_inc(sem("kc_ready"), 1)
                    else:
                        dve.wait_ge(sem("zeros_ready"), 1)
                        for hh in range(4):
                            rows_ = slice(32 * hh, 32 * hh + 32)
                            ins = dve.tensor_copy(v_bd[rows_, :, DH * hh:DH * hh + DH],
                                                  bank[5][rows_, 0:256].rearrange("p (g d) -> p g d", g=NG))
                            tick(ins) if hh < 3 else ins.then_inc(sem("v_bd_ready"), 1)
                if k == "glu":
                    gi = item["gi"]
                    if item["j"] == 0:
                        dve.memset(v_t[:, :, 0:2], 0.0).then_inc(sem("v_t_ready"), 1)
                    for tt in range(TT):
                        dve.wait_ge(sem("sg_ready"), 2 * gi + tt + 1)
                        dve.scalar_tensor_tensor(glu_a[:, tt, :], bank[tt][:, GC:2 * GC], rstd[:, tt:tt + 1], glu_s[:, tt, :],
                                                 ALU.mult, ALU.mult).then_inc(sem("act_ready"), 1)
                if k == "ffn":
                    f = item["f"]

                    def step(jb, i=None):
                        two = lambda a: 0 if i is None else a * 2 * i

                        def next_lo(q):
                            u = item["unit"] + (2 + 3 * (jb - 1) if jb else 0) + q + RING
                            if u >= len(units) or u < item["have"]:
                                return
                            lo_split(u, unit_raw[u], two)

                        if jb < NJ:
                            next_lo(0)
                            for tt in range(TT):
                                dve.wait_ge(sem("sg_ready"), 2 * (item["gi"] + jb) + tt + 1 + two(2))
                                dve.scalar_tensor_tensor(glu_a[:, tt, :], bank[tt][:, GC:2 * GC], rstd[:, tt:tt + 1] if f else 1.0,
                                                         glu_s[:, tt, :], ALU.mult, ALU.mult).then_inc(sem("act_ready"), 1)
                            if jb < NJ - 1:
                                for q in ([1, 2] if jb else [1]):
                                    next_lo(q)
                            tg = item["tg"] + jb
                            dve.wait_ge(sem("hi_t"), item["hl"] + jb + 1 + two(1))
                            dve.tensor_tensor(f_lo[:, jb % 2, :, :].rearrange("p a b -> p (a b)"), bank[6 + tg % 2][:, :],
                                              f_hi[:, jb % 2, :, :].rearrange("p a b -> p (a b)").bitcast(F32), ALU.subtract)\
                               .then_inc(sem(f"t_free{tg % 2}"), 1)
                            if jb == NJ - 1:
                                for q in (1, 2):
                                    next_lo(q)
                        else:
                            for nb in range(2):
                                for tt in range(TT):
                                    if 2 * nb + tt < 3:
                                        dve.wait_ge(sem("d_done"), 3 * f + 2 * nb + tt + 1)
                                    else:
                                        dve.wait_ge(sem("unit_used"), item["unit"] + 3 * NJ)
                                    update(tt, nb, bank[2 + 2 * tt + nb][:, :], "half" if f else 1)

                    first, turns = ffn_loop()
                    for j in range(first):
                        step(j)
                    with dve.Fori(0, turns) as i:
                        for h in range(2):
                            step(first + h, i)
                    for j in range(first + 2 * turns, NJ + 1):
                        step(j)
                    u = item["unit"] + 3 * NJ - 1 + RING
                    if u < len(units):
                        after_norm.append(u)

        @block.tensor
        def _(pe):
            def free_pairs(item):
                for q, n in enumerate(item["pairs_before"]):
                    if n:
                        pe.wait_ge(sem(f"pair_free{q}"), n)

            def three(dst, hi, lo, whi, wlo, start, stop):
                pe.matmul(dst, hi, whi, start=start, stop=False)
                pe.matmul(dst, hi, wlo, start=False, stop=False)
                return pe.matmul(dst, lo, whi, start=False, stop=stop)

            def glu_unit(u, half_, need=None, two=lambda a: 0):
                pe.wait_ge(sem("raw_done"), u + 1 + two(3))
                for kk in range(4):
                    kt = 4 * half_ + kk
                    if need is not None and kt % 2 == 0:
                        wait_group(pe, need[str(kt)])
                    wv = [r_[:, u % RING, 512 * kk:512 * kk + 512] for r_ in (w_hi, w_lo)]
                    for tt in range(TT):
                        ins = three(bank[tt][:, :], h_hi[:, kt, tt * P:(tt + 1) * P], h_lo[:, kt, tt * P:(tt + 1) * P],
                                    wv[0], wv[1], kt == 0, kt == KT - 1)
                return ins

            def glu_transposes(tg, gi, two=lambda a: 0, one=0):
                if tg >= 2:
                    pe.wait_ge(sem(f"t_free{tg % 2}"), tg // 2 + one)
                for tt in range(TT):
                    pe.wait_ge(sem("act_ready"), 2 * gi + tt + 1 + two(2))
                    for kk in range(2):
                        ins = pe.transpose(bank[6 + tg % 2][:, kk * T + tt * P:kk * T + (tt + 1) * P],
                                           glu_a[:, tt, kk * P:(kk + 1) * P], ident)
                ins.then_inc(sem("t_done"), 1)

            for item in plan:
                k = item["kind"]
                if k == "init":
                    pe.wait_ge(sem("const_full"), 16)
                    pe.wait_ge(sem("c_full"), 16 * 2)
                    pe.transpose(bank[5][:, 0:KT], rows2[0:KT, :], ident[0:KT, 0:KT]).then_inc(sem("c_t_done"), 1)
                    pe.transpose(bank[4][:, P:P + 56], rows2[0:56, :], ident[0:56, 0:56])
                    pe.wait_ge(sem("rows_full"), 16 * 7)
                    pe.transpose(bank[4][:, 0:P], rows1[:, :], ident).then_inc(sem("init_done"), 1)
                if k == "lin":
                    st, c, part, u, pi = item["stage"], item["chunk"], item["part"], item["unit"], item["pi"]
                    sub, subs = item.get("sub", 0), item.get("subs", 1)
                    pe.wait_ge(sem("raw_done"), u + 1)
                    b = [bank[2 * (pi % 2) + tt] for tt in range(TT)]
                    if part == 0 and sub == 0:
                        if item["pair_before"]:
                            pe.wait_ge(sem(f"pair_free{pi % 2}"), item["pair_before"])
                    if st == "cm":
                        pe.wait_ge(sem("xp_ready"), c + 1)
                        if part == 0:
                            pe.wait_ge(sem("small_full"), 16 * 4)
                            pe.matmul(b[0][0:60, 0:256], ones[0:1, 0:60], b1r[0:1, c, :], start=True, stop=False)
                        for kk in range(8):
                            kt = 8 * part + kk
                            wv = [r_[:, u % RING, 256 * kk:256 * kk + 256] for r_ in (w_hi, w_lo)]
                            ins = three(b[0][0:60, 0:256], xp_hi[:, kt, :], xp_lo[:, kt, :], wv[0], wv[1], False, kt == 15)
                        ins.then_inc(sem("unit_used"), 1)
                        continue
                    n = {"ki": 72, "gn": 48}.get(st, 512)
                    k0 = {"ba": 0, "bb": 4}.get(st, 4 * part)
                    kts = range(KT) if n < 512 else range(k0, k0 + 4)
                    single = st in ("ki", "gn", "ba", "bb")
                    for q, kt in enumerate(kts):
                        if q * subs // len(kts) != sub:
                            continue
                        if kt % 2 == 0:
                            wait_group(pe, item["need"][str(kt)])
                        wv = [r_[:, u % RING, n * q:n * q + n] for r_ in (w_hi, w_lo)]
                        for tt in range(TT):
                            first_ = q == 0 and (single or part == 0)
                            last_ = q == len(kts) - 1 and (single or part == 1)
                            ins = three(b[tt][:, 0:n], h_hi[:, kt, tt * P:(tt + 1) * P], h_lo[:, kt, tt * P:(tt + 1) * P],
                                        wv[0], wv[1], first_, last_)
                    if sub == subs - 1:
                        ins.then_inc(sem("unit_used"), 1)
                if k == "tp":
                    st, tg, g = item["stage"], item["tg"], item["g"]
                    b = bank[6 + tg % 2]
                    wait_bank(pe, tg)
                    if "outputs" in item:
                        pe.wait_ge(sem("o_ready"), item["outputs"])
                    if st == "mod" and find["mod", g][0] == "pe":
                        pe.wait_ge(sem("c_ready"), 1)
                        halves = [find["raw", g] - 1, find["raw", g]]
                        for r in halves:
                            pe.wait_ge(sem(f"early_full{r}"), 16)
                        for q in range(4):
                            for kt in range(KT):
                                ins = pe.matmul(b[:, q:q + 1], early[halves[kt // 4]][:, kt % 4, q * P:(q + 1) * P],
                                                c_act[:, kt:kt + 1], start=kt == 0, stop=kt == KT - 1)
                    elif st == "mod":
                        by, of = find["mod", g]
                        pe.wait_ge(sem("mod_used_" + by), of + 1)
                        a = acc[:, g % 2, :]
                        if g // 2 in (2, 5):
                            i5 = g // 2 // 3
                            pe.wait_ge(sem("b_row_full"), 16 * (i5 + 1))
                            pe.matmul(b[:, :], ones, a, start=True, stop=False)
                            ins = pe.matmul(b[:, :], ones[0:1, :], b_row[0:1, 512 * (g % 2):512 * (g % 2) + 512],
                                            start=False, stop=True)
                        else:
                            for q in range(4):
                                ins = pe.matmul(b[:, q:q + 1], a[:, q * P:(q + 1) * P], ones[:, 0:1], start=True, stop=True)
                    elif st in ("norm", "normf", "o", "merged", "on"):
                        if st == "norm":
                            pe.wait_ge(sem("x_ready"), 4 * xu[item["norm"]] - (2 if g < 2 else 0))
                            src = x
                        elif st == "normf":
                            pe.wait_ge(sem("xn_ready"), 2 * (item["norm"] + 1))
                            src = o1
                        elif st == "o":
                            pe.wait_ge(sem("o_ready"), 16)
                            src = o1
                        elif st == "on":
                            pe.wait_ge(sem("o_ready"), 80)
                            src = o2
                        else:
                            for c_ in range(2):
                                wait_pair(pe, find["pi", "bb", c_])
                            src = sig[:, :, 0, :]
                        for kk in range(2):
                            for tt in range(TT):
                                at = (2 * g + kk) * P
                                ins = pe.transpose(b[:, kk * T + tt * P:kk * T + (tt + 1) * P], src[:, tt, at:at + P], ident)
                    elif st in ("qb", "kb", "qa", "ka", "qi"):
                        pe.wait_ge(sem("rope_done"), ("qi", "qb", "kb", "qa", "ka").index(st) + 1)
                        for kk in range(2):
                            for tt in range(TT):
                                at = (2 * g + kk) * P
                                ins = pe.transpose(b[:, kk * T + tt * P:kk * T + (tt + 1) * P], ro[:, tt, at:at + P], ident)
                    elif st == "ki":
                        pe.wait_ge(sem("kid_ready"), 1)
                        for tt in range(TT):
                            ins = pe.transpose(b[:, tt * P:(tt + 1) * P], kid[:, tt, :], ident)
                    elif st == "cb":
                        wait_pair(pe, find["pi", "cb", g // 2])
                        for kk in range(2):
                            for tt in range(TT):
                                at = (2 * g + kk) * P
                                ins = pe.transpose(b[:, kk * T + tt * P:kk * T + (tt + 1) * P], b_s[:, tt, at:at + P], ident)
                    elif st == "kvt":
                        if item["c"] == 0:
                            wait_pair(pe, find["pi", "kv", 0])
                            s_, g0 = divmod(2 * g, NG)
                            srcs = [kv_d[:, tt, s_, g0 + kk, :, :] for kk in range(2) for tt in range(TT)]
                        else:
                            pe.wait_ge(sem("kd_done"), item["c"])
                            srcs = [kd[:, tt, 2 * g + kk, :, :] for kk in range(2) for tt in range(TT)]
                        for q, s_ in enumerate(srcs):
                            ins = pe.transpose(b[:, q * P:(q + 1) * P], s_.rearrange("p a b -> p (a b)"), ident)
                    elif st == "qn":
                        wait_pair(pe, find["pi", "qg", item["c"]])
                        for kk in range(2):
                            for tt in range(TT):
                                at = (2 * g + kk) * P
                                ins = pe.transpose(b[:, kk * T + tt * P:kk * T + (tt + 1) * P], pqn[:, tt, at:at + P], ident)
                    elif st == "hc":
                        wait_pair(pe, find["pi", "cm", item["c"]])
                        for kk in range(2):
                            ins = pe.transpose(b[:, kk * 60:(kk + 1) * 60], hc[0:60, kk * P:(kk + 1) * P], ident[0:60, 0:60])
                    elif st == "kc":
                        pe.wait_ge(sem("kc_ready"), 1)
                        ins = pe.transpose(b[:, 0:60], kc[0:60].rearrange("p a b -> p (a b)"), ident[0:60, 0:60])
                    elif st == "pc":
                        pe.wait_ge(sem("pc_ready"), item["tt"] + 1)
                        for g_ in range(NG):
                            ins = pe.transpose(b[:, g_ * P:(g_ + 1) * P], pc[:, 4 * g_:4 * g_ + 4, :].rearrange("p a b -> p (a b)"), ident)
                    elif st == "p":
                        pe.wait_ge(sem("exp_done"), item["it"] + 1)
                        if item["it"] >= 2:
                            pe.wait_ge(sem("o_ready"), item["it"] - 1)
                        for kk in range(item["tt"] + 1):
                            ins = pe.transpose(b[:, kk * P:(kk + 1) * P], p_s[:, item["it"] % 2, kk * P:(kk + 1) * P], ident)
                    ins.then_inc(sem("t_done"), 1)
                if k == "ix":
                    n, tt, pr = P * (item["tt"] + 1), item["tt"], item["pair"]
                    if item["n"]:
                        pe.wait_ge(sem("rl_ready"), 2 * item["n"])
                    for hh in range(2):
                        r_ = slice(64 * hh, 64 * hh + 64)
                        ins = pe.matmul(bank[4 + hh][:, 0:n], qi_t[r_, pr, tt * P:(tt + 1) * P], ki_t[r_, 0:n], start=True, stop=True)
                    ins.then_inc(sem("ix_done"), 1)
                if k == "qk":
                    it, tt, h = item["it"], item["tt"], item["h"]
                    n = P * (tt + 1)
                    if it == 0:
                        pe.wait_ge(sem("rl_ready"), 16)
                    if it == 16:
                        pe.wait_ge(sem("oc_ready"), 2)
                    if it >= 2:
                        pe.wait_ge(sem("sm_done"), it - 1)
                    if it in (0, 8):
                        for st in ("qb", "kb") if it == 0 else ("qa", "ka"):
                            for g in range(2):
                                wait_group(pe, find["tg", st, g])
                    if item["b"] in ("dsa", "moba"):
                        lhs, rhs = q_t[:, h, tt * P:(tt + 1) * P], k_t[:, h, 0:n]
                    else:
                        r_ = slice(64 * (h % 2), 64 * (h % 2) + 64)
                        br = 0 if item["b"] == "sel" else 1
                        lhs, rhs = q_n[r_, h // 2, tt * P:(tt + 1) * P], kn_t[r_, br, h // 4, 0:n]
                    pe.matmul(bank[4 + it % 2][:, 0:n], lhs, rhs, start=True, stop=True).then_inc(sem("qk_done"), 1)
                if k == "pv":
                    it, tt, h = item["it"], item["tt"], item["h"]
                    wait_group(pe, find["tg", "p", it])
                    if item["b"] in ("dsa", "moba"):
                        if it in (0, 8):
                            wait_pair(pe, find["pi", "vb" if it == 0 else "va", 0])
                        wv = lambda kk: v_s[:, kk, HD * h:HD * h + HD]
                        w_ = HD
                    else:
                        br = 0 if item["b"] == "sel" else 1
                        wv = lambda kk: vn_s[:, br, kk, DH * (h // 4):DH * (h // 4) + DH]
                        w_ = DH
                    for kk in range(tt + 1):
                        ins = pe.matmul(bank[6 + find["tg", "p", it] % 2][:, T:T + w_], pt_s[:, it % 2, kk * P:(kk + 1) * P], wv(kk),
                                        start=kk == 0, stop=kk == tt)
                    ins.then_inc(sem("pv_done"), 1)
                if k == "cmp":
                    wait_group(pe, find["tg", "hc", (item["s"], 0)])
                    if item["s"] == 0:
                        for kk in range(2):
                            ins = pe.matmul(bank[4][0:60, 0:DH], hc_t[:, kk, :], w2[:, 0, kk, :], start=kk == 0, stop=kk == 1)
                    else:
                        for g in range(NG):
                            for kk in range(2):
                                ins = pe.matmul(bank[5][:, DH * g:DH * g + DH], hc_p[:, kk, g, :, :].rearrange("p a b -> p (a b)"),
                                                w2[:, 1, kk, :], start=kk == 0, stop=kk == 1)
                    ins.then_inc(sem("cmp_done"), 1)
                if k == "cs":
                    tt = item["tt"]
                    if tt == 0:
                        wait_group(pe, find["tg", "kc", 0])
                        for g in range(2):
                            wait_group(pe, find["tg", "qn", (1, g)])
                        pe.wait_ge(sem("v_bd_ready"), 1)
                        pe.wait_ge(sem("kc_ready"), 1)
                    else:
                        pe.wait_ge(sem("oc_ready"), tt)
                    for h in range(NQ):
                        r_ = slice(64 * (h % 2), 64 * (h % 2) + 64)
                        g = h // 4
                        ins = pe.matmul(bank[4 + h % 2][:, 16 * (h // 2):16 * (h // 2) + NC], q_n[r_, h // 2, tt * P:(tt + 1) * P],
                                        kc_t[r_, NC * g:NC * g + NC], start=True, stop=True)
                    ins.then_inc(sem("cs_done"), 1)
                if k == "co_":
                    tt = item["tt"]
                    wait_group(pe, find["tg", "pc", (tt, 0)])
                    for g in range(NG):
                        ins = pe.matmul(bank[4 + g // 2][:, 256 * (g % 2):256 * (g % 2) + 256], pc_t[:, g, :], v_bd[:, g, :],
                                        start=True, stop=True)
                    ins.then_inc(sem("cv_done"), 1)
                if k == "glu":
                    u, gi = item["unit"], item["gi"]
                    if item["j"] == 0:
                        free_pairs(item)
                    glu_unit(u, 0, item["need"] if item["j"] == 0 else None).then_inc(sem("unit_used"), 1)
                    glu_unit(u + 1, 1, item["need"] if item["j"] == 0 else None).then_inc(sem("unit_used"), 1)
                    glu_transposes(item["tg"], gi)
                if k == "ffn":
                    f = item["f"]

                    def step(jb, i=None):
                        two = lambda a: 0 if i is None else a * 2 * i
                        u = item["unit"] + (2 + 3 * (jb - 1) if jb else 0)
                        if jb < NJ:
                            need = item["need"] if jb == 0 else None
                            glu_unit(u, 0, need, two).then_inc(sem("unit_used"), 1)
                            glu_unit(u + 1, 1, need, two).then_inc(sem("unit_used"), 1)
                            u += 2
                        if jb > 0:
                            tg = item["tg"] + jb - 1
                            pe.wait_ge(sem("raw_done"), u + 1 + two(3))
                            pe.wait_ge(sem(f"t_free{tg % 2}"), tg // 2 + 1 + (0 if i is None else i))
                            fb = (jb - 1) % 2
                            order = [(nb, tt) for nb in range(2) for tt in range(TT)] if jb == NJ else \
                                    [(nb, tt) for tt in range(TT) for nb in range(2)]
                            if jb == NJ:
                                for n_, (nb, tt) in enumerate(order):
                                    for kk in range(2):
                                        ins = three(bank[2 + 2 * tt + nb][:, :], f_hi[:, fb, kk, tt * P:(tt + 1) * P], f_lo[:, fb, kk, tt * P:(tt + 1) * P],
                                                    w_hi[:, u % RING, D * kk + 512 * nb:D * kk + 512 * nb + 512],
                                                    w_lo[:, u % RING, D * kk + 512 * nb:D * kk + 512 * nb + 512], False, kk == 1)
                                    ins.then_inc(sem("d_done" if n_ < 3 else "unit_used"), 1)
                            else:
                                for kk in range(2):
                                    for nb, tt in order:
                                        ins = three(bank[2 + 2 * tt + nb][:, :], f_hi[:, fb, kk, tt * P:(tt + 1) * P], f_lo[:, fb, kk, tt * P:(tt + 1) * P],
                                                    w_hi[:, u % RING, D * kk + 512 * nb:D * kk + 512 * nb + 512],
                                                    w_lo[:, u % RING, D * kk + 512 * nb:D * kk + 512 * nb + 512], jb == 1 and kk == 0, False)
                                ins.then_inc(sem("unit_used"), 1)
                        if jb < NJ:
                            glu_transposes(item["tg"] + jb, item["gi"] + jb, two, 0 if i is None else i)

                    free_pairs(item)
                    first, turns = ffn_loop()
                    for j in range(first):
                        step(j)
                    with pe.Fori(0, turns) as i:
                        for h in range(2):
                            step(first + h, i)
                    for j in range(first + 2 * turns, NJ + 1):
                        step(j)


_INS = ["x", "c", "w_mod", "b_mod", "g_mix_norm", "g_ffn_norm", "w_in", "g_q_dsa", "g_k_dsa", "g_q_moba", "g_k_moba",
        "w_br_dsa", "w_br_moba", "w_out", "w_gate_up", "w_down", "ffn_norm_2", "ffn_w_gate_up_2", "ffn_w_down_2",
        "mix_norm_2", "conv_w_in_2", "conv_w_2", "conv_w_out_2", "kv_norm_2", "kv_w_2", "cmp_pos_2", "cmp_w1_2",
        "cmp_b1_2", "cmp_w2_2", "k_norm_2", "nsa_w_qg_2", "q_norm_2", "nsa_w_o_2"]


def kernel(**inputs):
    import numpy as _np
    import concourse.bacc as _bacc
    from concourse import mybir as _mybir
    from concourse.bass_utils import run_bass_kernel_spmd as _run

    nc = _bacc.Bacc("TRN2", target_bir_lowering=False, num_devices=1)
    arrays, args = {}, {}
    for name in _INS:
        a = _np.ascontiguousarray(inputs[name])
        arrays[f"in_{name}_dram"] = a
        args[name] = nc.dram_tensor(f"in_{name}_dram", a.shape, _mybir.dt.from_np(a.dtype), kind="ExternalInput").ap()
    arrays["const_dram"] = constant_table()
    args["const"] = nc.dram_tensor("const_dram", (P, C_END), F32, kind="ExternalInput").ap()
    out = nc.dram_tensor("out_0_dram", (T, D), F32, kind="ExternalOutput").ap()
    two_block_program(nc, args, out)
    r = _run(nc, [arrays], core_ids=[0])
    return r.results[0]["out_0_dram"].reshape(1, T, D)
```
